# Optimizing a Trainium2 kernel written in Bass

```python
import math
import jax, jax.numpy as jnp
from jax import lax
import numpy as np

D_MODEL = 1024
BATCH = 1
SEQ = 512
DEPTH = 2

HEAD_DIM = 64
SSD_WIDTH = D_MODEL // 2
SSD_HEADS = SSD_WIDTH // HEAD_DIM
SSD_GROUPS = 2
SSD_STATE = 128
SSD_CONV = 4
SSD_CHUNK = 128
SSD_CONV_DIM = SSD_WIDTH + 2 * SSD_GROUPS * SSD_STATE
SB_WIDTH = D_MODEL // 4
SB_HEADS = SB_WIDTH // HEAD_DIM
SB_BLOCK = 128
NSA_WIDTH = D_MODEL // 4
NSA_HEADS = NSA_WIDTH // HEAD_DIM
CMP_LEN = 32
CMP_STRIDE = 16
SEL_BLOCK = 64
SEL_TOPK = 16
WINDOW = 512
NSA_QBLOCK = 128
FORCE_SCORE = 1e9
MIX_WIDTH = SSD_WIDTH + SB_WIDTH + NSA_WIDTH
ROT_DIM = HEAD_DIM // 4
ROPE_THETA = 500000.0
PEER_HEADS = 8
N_KEYS = 128
N_EXPERTS = N_KEYS * N_KEYS
PEER_TOPK = 16
PEER_QDIM = 256
PEER_TOKEN_BLOCK = 128
NORM_EPS = 1e-6
IN_SIZES = (SSD_WIDTH, SSD_CONV_DIM, SSD_HEADS, 3 * SB_WIDTH, NSA_WIDTH, 6 * HEAD_DIM, 3 * NSA_HEADS)
IN_DIM = sum(IN_SIZES)
IN_SPLITS = tuple(sum(IN_SIZES[:i + 1]) for i in range(len(IN_SIZES) - 1))

kernel_name = "hybrid_ssd_stickbreak_nsa_peer"

def rms_norm(x, w):
    xf = x.astype(jnp.float32)
    y = xf * lax.rsqrt(jnp.mean(xf * xf, axis=-1, keepdims=True) + NORM_EPS)
    return (y * w.astype(jnp.float32)).astype(x.dtype)

def rope_tables(seq_len):
    pos = jnp.arange(seq_len, dtype=jnp.float32)
    inv_freq = ROPE_THETA ** (-jnp.arange(0, ROT_DIM, 2, dtype=jnp.float32) / ROT_DIM)
    ang = pos[:, None] * inv_freq[None, :]
    return jnp.cos(ang), jnp.sin(ang)

def partial_rope(x, cos, sin):
    half = ROT_DIM // 2
    x1, x2, rest = x[..., :half], x[..., half:ROT_DIM], x[..., ROT_DIM:]
    c, s = cos.astype(x.dtype), sin.astype(x.dtype)
    return jnp.concatenate([x1 * c - x2 * s, x2 * c + x1 * s, rest], axis=-1)

def causal_depthwise_conv(x, w):
    return lax.conv_general_dilated(
        x, w[:, None, :], window_strides=(1,), padding=[(w.shape[0] - 1, 0)],
        dimension_numbers=('NWC', 'WIO', 'NWC'), feature_group_count=x.shape[-1])

def segsum(x):
    T = x.shape[-1]
    xr = jnp.broadcast_to(x[..., :, None], x.shape + (T,))
    strict = jnp.tril(jnp.ones((T, T), dtype=bool), -1)
    ss = jnp.cumsum(jnp.where(strict, xr, 0.0), axis=-2)
    return jnp.where(jnp.tril(jnp.ones((T, T), dtype=bool)), ss, -jnp.inf)

def ssd_mixer(z, xbc, dt_raw, conv_w, conv_b, dt_bias, a_log, d_skip, norm_w):
    Bsz, S, _ = z.shape
    G, R, P, N, L = SSD_GROUPS, SSD_HEADS // SSD_GROUPS, HEAD_DIM, SSD_STATE, SSD_CHUNK
    nc = S // L
    xbc = jax.nn.silu(causal_depthwise_conv(xbc, conv_w) + conv_b)
    xs, b_in, c_in = jnp.split(xbc, [SSD_WIDTH, SSD_WIDTH + G * N], axis=-1)
    dt = jax.nn.softplus((dt_raw + dt_bias).astype(jnp.float32))
    a = -jnp.exp(a_log.astype(jnp.float32))
    xh = xs.reshape(Bsz, S, SSD_HEADS, P)
    X = (xh * dt[..., None]).reshape(Bsz, nc, L, G, R, P)
    Bm = b_in.reshape(Bsz, nc, L, G, N)
    Cm = c_in.reshape(Bsz, nc, L, G, N)
    A = (dt * a).reshape(Bsz, nc, L, G, R).transpose(0, 3, 4, 1, 2)
    A_cs = jnp.cumsum(A, axis=-1)
    Lmat = jnp.exp(segsum(A))
    CB = jnp.einsum('bclgn,bcsgn->bgcls', Cm, Bm)
    y_diag = jnp.einsum('bgrcls,bcsgrp->bclgrp', Lmat * CB[:, :, None], X)
    decay_states = jnp.exp(A_cs[..., -1:] - A_cs).transpose(0, 3, 4, 1, 2)
    states = jnp.einsum('bclgn,bclgrp->bcgrpn', Bm, X * decay_states[..., None])
    states = jnp.concatenate([jnp.zeros_like(states[:, :1]), states], axis=1)
    A_last = jnp.pad(A_cs[..., -1], ((0, 0), (0, 0), (0, 0), (1, 0)))
    decay_chunk = jnp.exp(segsum(A_last))
    states = jnp.einsum('bgrzc,bcgrpn->bzgrpn', decay_chunk, states)[:, :-1]
    y_off = jnp.einsum('bclgn,bcgrpn->bclgrp', Cm, states) * jnp.exp(A_cs).transpose(0, 3, 4, 1, 2)[..., None]
    y = (y_diag + y_off).reshape(Bsz, S, SSD_HEADS, P) + xh * d_skip[:, None]
    y = y.reshape(Bsz, S, SSD_WIDTH)
    return rms_norm(y * jax.nn.silu(z), norm_w)

def stick_breaking_attention(qkv):
    Bsz, S, _ = qkv.shape
    H, d = SB_HEADS, HEAD_DIM
    q, k, v = [u.reshape(Bsz, S, H, d).transpose(0, 2, 1, 3) for u in jnp.split(qkv, 3, axis=-1)]
    nqb = S // SB_BLOCK
    q_blocks = q.reshape(Bsz, H, nqb, SB_BLOCK, d).transpose(2, 0, 1, 3, 4)
    starts = jnp.arange(nqb) * SB_BLOCK
    kpos = jnp.arange(S)
    scale = d ** -0.5

    def block(args):
        qi, t0 = args
        tq = t0 + jnp.arange(SB_BLOCK)
        mask = kpos[None, :] < tq[:, None]
        z = (jnp.einsum('bhqd,bhkd->bhqk', qi, k) * scale).astype(jnp.float32)
        log_beta = jnp.where(mask, jax.nn.log_sigmoid(z), -jnp.inf)
        log_stay = jnp.where(mask, jax.nn.log_sigmoid(-z), 0.0)
        log_after = lax.cumsum(log_stay, axis=log_stay.ndim - 1, reverse=True) - log_stay
        w = jnp.exp(log_beta + log_after)
        return jnp.einsum('bhqk,bhkd->bhqd', w.astype(v.dtype), v)

    o = lax.map(block, (q_blocks, starts))
    return o.transpose(1, 0, 3, 2, 4).reshape(Bsz, S, H * d)

def nsa_attention(q, kv, gate_logits, q_norm_w, k_norm_w, cmp_pos, cmp_w, cos, sin):
    Bsz, S, _ = q.shape
    H, d = NSA_HEADS, HEAD_DIM
    scale = d ** -0.5
    t = jnp.arange(S)
    kc, vc, ks, vs, kw, vw = jnp.split(kv, 6, axis=-1)
    q = partial_rope(rms_norm(q.reshape(Bsz, S, H, d), q_norm_w).transpose(0, 2, 1, 3), cos, sin)

    n_cmp = (S - CMP_LEN) // CMP_STRIDE + 1
    cmp_start = np.arange(n_cmp) * CMP_STRIDE
    tok = cmp_start[:, None] + np.arange(CMP_LEN)[None, :]
    kc_blk = (partial_rope(kc, cos, sin)[:, tok] + cmp_pos[0]).reshape(Bsz, n_cmp, CMP_LEN * d)
    k_cmp = rms_norm(kc_blk @ cmp_w[0], k_norm_w[0])
    v_cmp = (vc[:, tok] + cmp_pos[1]).reshape(Bsz, n_cmp, CMP_LEN * d) @ cmp_w[1]
    cmp_visible = jnp.asarray(cmp_start + CMP_LEN - 1)[None, :] <= t[:, None]
    s_cmp = (jnp.einsum('bhsd,bcd->bhsc', q, k_cmp) * scale).astype(jnp.float32)
    p_cmp = jax.nn.softmax(jnp.where(cmp_visible, s_cmp, -1e30), axis=-1) * cmp_visible
    o_cmp = jnp.einsum('bhsc,bcd->bhsd', p_cmp.astype(v_cmp.dtype), v_cmp)

    n_sel = S // SEL_BLOCK
    sel_start = np.arange(n_sel) * SEL_BLOCK
    overlap = ((cmp_start[:, None] < sel_start[None, :] + SEL_BLOCK)
               & (cmp_start[:, None] + CMP_LEN > sel_start[None, :])).astype(np.float32)
    imp = jnp.einsum('bhsc,cj->bsj', p_cmp, jnp.asarray(overlap))
    j = jnp.arange(n_sel)[None, :]
    blk_t = (t // SEL_BLOCK)[:, None]
    forced = (j == 0) | (j == blk_t) | (j == blk_t - 1)
    causal = j * SEL_BLOCK <= t[:, None]
    imp = jnp.where(causal, jnp.where(forced, FORCE_SCORE, imp), -jnp.inf)
    n_top = min(SEL_TOPK, n_sel)
    _, sel_idx = lax.top_k(imp, n_top)

    ks = partial_rope(rms_norm(ks, k_norm_w[1]), cos, sin)
    kw = partial_rope(rms_norm(kw, k_norm_w[2]), cos, sin)
    ks_blk = ks.reshape(Bsz, n_sel, SEL_BLOCK, d)
    vs_blk = vs.reshape(Bsz, n_sel, SEL_BLOCK, d)
    kw_pad = jnp.pad(kw, ((0, 0), (WINDOW, 0), (0, 0)))
    vw_pad = jnp.pad(vw, ((0, 0), (WINDOW, 0), (0, 0)))
    nqb = S // NSA_QBLOCK
    q_blocks = q.reshape(Bsz, H, nqb, NSA_QBLOCK, d).transpose(2, 0, 1, 3, 4)
    idx_blocks = sel_idx.reshape(Bsz, nqb, NSA_QBLOCK, n_top).transpose(1, 0, 2, 3)
    starts = jnp.arange(nqb) * NSA_QBLOCK
    take_blocks = jax.vmap(lambda blocks, idx: blocks[idx])
    n_win = WINDOW + NSA_QBLOCK

    def block(args):
        qi, idx, t0 = args
        tq = t0 + jnp.arange(NSA_QBLOCK)
        k_g = take_blocks(ks_blk, idx).reshape(Bsz, NSA_QBLOCK, n_top * SEL_BLOCK, d)
        v_g = take_blocks(vs_blk, idx).reshape(Bsz, NSA_QBLOCK, n_top * SEL_BLOCK, d)
        kpos = (idx[..., None] * SEL_BLOCK + jnp.arange(SEL_BLOCK)).reshape(Bsz, NSA_QBLOCK, n_top * SEL_BLOCK)
        m_sel = (kpos <= tq[None, :, None])[:, None]
        s_sel = (jnp.einsum('bhqd,bqkd->bhqk', qi, k_g) * scale).astype(jnp.float32)
        p_sel = jax.nn.softmax(jnp.where(m_sel, s_sel, -1e30), axis=-1)
        o_sel = jnp.einsum('bhqk,bqkd->bhqd', p_sel.astype(v_g.dtype), v_g)
        k_w = lax.dynamic_slice_in_dim(kw_pad, t0, n_win, axis=1)
        v_w = lax.dynamic_slice_in_dim(vw_pad, t0, n_win, axis=1)
        kpos_w = t0 - WINDOW + jnp.arange(n_win)
        rel = tq[:, None] - kpos_w[None, :]
        m_win = (rel >= 0) & (rel < WINDOW) & (kpos_w[None, :] >= 0)
        s_win = (jnp.einsum('bhqd,bkd->bhqk', qi, k_w) * scale).astype(jnp.float32)
        p_win = jax.nn.softmax(jnp.where(m_win, s_win, -1e30), axis=-1)
        o_win = jnp.einsum('bhqk,bkd->bhqd', p_win.astype(v_w.dtype), v_w)
        return o_sel, o_win

    o_sel, o_win = lax.map(block, (q_blocks, idx_blocks, starts))
    unblock = lambda o: o.transpose(1, 2, 0, 3, 4).reshape(Bsz, H, S, d)
    g = jax.nn.sigmoid(gate_logits.reshape(Bsz, S, H, 3).astype(jnp.float32)).transpose(0, 2, 1, 3)
    o = g[..., 0:1] * o_cmp + g[..., 1:2] * unblock(o_sel) + g[..., 2:3] * unblock(o_win)
    return o.transpose(0, 2, 1, 3).reshape(Bsz, S, NSA_WIDTH)

def peer_ffn(h, w_q, sub_keys, u_tab, v_tab):
    Bsz, S, D = h.shape
    T = Bsz * S
    Tb = PEER_TOKEN_BLOCK
    half = PEER_QDIM // 2

    def block(xb):
        q = (xb @ w_q).reshape(Tb, PEER_HEADS, 2, half)
        s = jnp.einsum('thpd,pkd->thpk', q, sub_keys).astype(jnp.float32)
        sv, si = lax.top_k(s, PEER_TOPK)
        cand = sv[:, :, 0, :, None] + sv[:, :, 1, None, :]
        cv, ci = lax.top_k(cand.reshape(Tb, PEER_HEADS, PEER_TOPK * PEER_TOPK), PEER_TOPK)
        i1 = jnp.take_along_axis(si[:, :, 0, :], ci // PEER_TOPK, axis=-1)
        i2 = jnp.take_along_axis(si[:, :, 1, :], ci % PEER_TOPK, axis=-1)
        eidx = i1 * N_KEYS + i2
        g = jax.nn.softmax(cv, axis=-1)
        u = u_tab[eidx]
        v = v_tab[eidx]
        a = jax.nn.gelu(jnp.einsum('thkd,td->thk', u, xb).astype(jnp.float32), approximate=False)
        return jnp.einsum('thk,thkd->td', (g * a).astype(v.dtype), v)

    out = lax.map(block, h.reshape(T // Tb, Tb, D))
    return out.reshape(Bsz, S, D)

def setup_inputs(seed: int = 0) -> dict:
    key = jax.random.key(seed)
    ks = jax.random.split(key, 24)
    L, D = DEPTH, D_MODEL
    nrm = lambda k, shape, scale: jax.random.normal(k, shape, jnp.float32) * scale
    dt0 = jnp.exp(jax.random.uniform(ks[5], (L, SSD_HEADS), jnp.float32, math.log(1e-3), math.log(1e-1)))
    return {
        "x": nrm(ks[0], (BATCH, SEQ, D), 1.0),
        "norm1_w": 1.0 + nrm(ks[1], (L, D), 0.02),
        "w_in": nrm(ks[2], (L, D, IN_DIM), D ** -0.5),
        "conv_w": nrm(ks[3], (L, SSD_CONV, SSD_CONV_DIM), SSD_CONV ** -0.5),
        "conv_b": nrm(ks[4], (L, SSD_CONV_DIM), 0.02),
        "dt_bias": dt0 + jnp.log(-jnp.expm1(-dt0)),
        "a_log": jnp.log(jax.random.uniform(ks[6], (L, SSD_HEADS), jnp.float32, 1.0, 16.0)),
        "d_skip": 1.0 + nrm(ks[7], (L, SSD_HEADS), 0.02),
        "ssd_norm_w": 1.0 + nrm(ks[8], (L, SSD_WIDTH), 0.02),
        "sb_out_w": 1.0 + nrm(ks[9], (L, SB_WIDTH), 0.02),
        "nsa_q_norm_w": 1.0 + nrm(ks[10], (L, HEAD_DIM), 0.02),
        "nsa_k_norm_w": 1.0 + nrm(ks[11], (L, 3, HEAD_DIM), 0.02),
        "nsa_cmp_pos": nrm(ks[12], (L, 2, CMP_LEN, HEAD_DIM), 0.1),
        "nsa_cmp_w": nrm(ks[13], (L, 2, CMP_LEN * HEAD_DIM, HEAD_DIM), (CMP_LEN * HEAD_DIM) ** -0.5),
        "nsa_out_w": 1.0 + nrm(ks[14], (L, NSA_WIDTH), 0.02),
        "w_out": nrm(ks[15], (L, MIX_WIDTH, D), MIX_WIDTH ** -0.5),
        "norm2_w": 1.0 + nrm(ks[16], (L, D), 0.02),
        "peer_w_q": nrm(ks[17], (L, D, PEER_HEADS * PEER_QDIM), D ** -0.5),
        "peer_sub_keys": nrm(ks[18], (L, 2, N_KEYS, PEER_QDIM // 2), (PEER_QDIM // 2) ** -0.5),
        "peer_u": nrm(ks[19], (L, N_EXPERTS, D), D ** -0.5),
        "peer_v": nrm(ks[20], (L, N_EXPERTS, D), (PEER_HEADS * PEER_TOPK) ** -0.5),
    }

def reference(x, norm1_w, w_in, conv_w, conv_b, dt_bias, a_log, d_skip, ssd_norm_w, sb_out_w,
              nsa_q_norm_w, nsa_k_norm_w, nsa_cmp_pos, nsa_cmp_w, nsa_out_w, w_out, norm2_w,
              peer_w_q, peer_sub_keys, peer_u, peer_v):
    cos, sin = rope_tables(x.shape[1])
    for l in range(DEPTH):
        h = rms_norm(x, norm1_w[l])
        proj = h @ w_in[l]
        z, xbc, dt_raw, sb_qkv, nsa_q, nsa_kv, nsa_gate = jnp.split(proj, IN_SPLITS, axis=-1)
        y_ssd = ssd_mixer(z, xbc, dt_raw, conv_w[l], conv_b[l], dt_bias[l], a_log[l], d_skip[l], ssd_norm_w[l])
        y_sb = rms_norm(stick_breaking_attention(sb_qkv), sb_out_w[l])
        y_nsa = rms_norm(nsa_attention(nsa_q, nsa_kv, nsa_gate, nsa_q_norm_w[l], nsa_k_norm_w[l],
                                       nsa_cmp_pos[l], nsa_cmp_w[l], cos, sin), nsa_out_w[l])
        mixed = jnp.concatenate([y_ssd, y_sb, y_nsa], axis=-1).astype(x.dtype) @ w_out[l]
        x = x + mixed
        x = x + peer_ffn(rms_norm(x, norm2_w[l]), peer_w_q[l], peer_sub_keys[l], peer_u[l], peer_v[l]).astype(x.dtype)
    return x


_drawn_inputs = setup_inputs


def setup_inputs(seed=0):
    import zlib

    import numpy as np

    out = dict(_drawn_inputs(seed))
    spreads = {}
    factors = {'conv_b': 2.833,
     'd_skip': 6.479,
     'ssd_norm_w': 3.981,
     'sb_out_w': 5.266,
     'nsa_q_norm_w': 5.759,
     'nsa_k_norm_w': 6.968,
     'nsa_out_w': 5.031,
     'norm2_w': 8.0}
    for name, (base, spread) in spreads.items():
        noise = np.random.default_rng([zlib.crc32(name.encode()), seed]).standard_normal(out[name].shape)
        drawn = base * np.exp(spread * noise) if base else spread * noise
        out[name] = __import__('jax').numpy.asarray(drawn.astype(out[name].dtype))
    for name, factor in factors.items():
        out[name] = (out[name] * factor).astype(out[name].dtype)
    return out
```

```python
from contextlib import ExitStack

import numpy as np
import concourse.bass as bass
from concourse import mybir

DEPTH, SEQ, D, P = 2, 512, 1024, 128
BLOCKS = SEQ // P
STEPS = DEPTH * BLOCKS
KT = D // P
HD = 64
SSD_W, SSD_H, SSD_N, TAPS = 512, 8, 128, 4
CONV_DIM = SSD_W + 4 * SSD_N
SB_H, NSA_H = 4, 4
IN_DIM = 2964
Z0, XS0, BC0, DT0, SBQ0, SBV0, KV0 = 0, 512, 1024, 1536, 1544, 2056, 2568
KVW = IN_DIM - KV0
CMP_LEN, CMP_STRIDE, CMP_PAD = 32, 16, 32
PEER_H, TOPK, KEYS, PEER_Q = 8, 16, 128, 2048
EXPERTS = KEYS * KEYS
SLOTS = PEER_H * TOPK
EPS = 1e-6
NEG = -1e30
SCALE = HD ** -0.5
U_RING, V_RING, DIAG_RING, W_RING = 5, 5, 3, 2
LAG = TOPK + 2

CONST = {}


def constants():
    i = np.arange(P)
    row, col = i[:, None], i[None, :]
    one, zero = np.ones((P, P)), np.zeros((P, P))
    pieces = {
        "ident": row == col,
        "tri": row <= col,
        "neg_tri_ge": -1.0 * (row >= col),
        "ones": one,
        "neg_ones": -one,
        "later": np.where(row > col, NEG, 0.0),
    }
    seen, unseen = [one] * (BLOCKS - 1), [zero] * (BLOCKS - 1)
    pieces["stay"] = np.concatenate([*seen, row < col, *unseen], 1)
    pieces["stay_neg"] = np.concatenate([*unseen, np.where(row < col, 0, NEG), *[NEG * one] * (BLOCKS - 1)], 1)
    pieces["causal_neg"] = np.concatenate([*unseen, np.where(col <= row, 0, NEG), *[NEG * one] * (BLOCKS - 1)], 1)
    last = np.arange(CMP_PAD) * CMP_STRIDE + CMP_LEN - 1
    token = np.arange(SEQ).reshape(BLOCKS, P).T[:, :, None, None]
    visible = np.broadcast_to(last[None, None, None, :] <= token, (P, BLOCKS, NSA_H, CMP_PAD)).reshape(P, -1)
    pieces["cmp_neg"] = np.where(visible, 0.0, NEG)
    pieces["cmp_seen"] = visible
    pieces["head_of"] = (row // CMP_PAD) == np.arange(NSA_H)[None, :]
    inv = np.float32(500000.0) ** (-np.arange(0, 16, 2, dtype=np.float32) / np.float32(16))
    angle = (np.arange(SEQ, dtype=np.float32)[:, None] * inv[None, :]).astype(np.float32)
    rope = np.concatenate([np.cos(angle), np.sin(angle)], 1).reshape(BLOCKS, P, 16)
    pieces["rope"] = rope.transpose(1, 0, 2).reshape(P, -1)
    pieces["iota"] = np.broadcast_to(np.arange(TOPK), (P, TOPK))
    steps = np.arange(STEPS)
    pieces["carry"] = np.broadcast_to(steps % BLOCKS != 0, (P, STEPS))
    pieces["first_row"] = np.broadcast_to(steps // BLOCKS * EXPERTS, (P, STEPS))
    at, parts = 0, []
    for name, piece in pieces.items():
        piece = np.asarray(piece, np.float32)
        CONST[name] = (at, at + piece.shape[1])
        at += piece.shape[1]
        parts.append(piece)
    return np.ascontiguousarray(np.concatenate(parts, 1))


PHASES = (
    ["params", "norm1", "norm1_t"]
    + [f"xs{i}" for i in range(2)] + [f"bc{i}" for i in range(2)]
    + ["conv0", "sbqk0", "conv1", "sbqk1", "conv2", "z0", "conv3", "z1", "conv_out", "vq0", "vq1", "kv0", "kv1"]
    + ["xs_t", "dt", "cumsum", "decay0", "decay1", "y_diag", "y_off", "y_sum"]
    + [f"sb{i}" for i in range(SB_H + 2)] + ["sb_norm", "nsa_norm", "nsa_rope", "nsa_t"]
    + [f"cmp{i}" for i in range(8)] + ["cmp_t", "cmp_norm", "cmp_kt", "cmp_s", "cmp_pt", "cmp_o"]
    + [f"att{i}" for i in range(2 * NSA_H + 2)] + ["nsa_sum", "mix_t"]
    + [f"out{i}" for i in range(4)] + ["norm2", "norm2_t"]
    + ["q0a", "q0b", "q0t", "q1a", "q1b", "q0s", "q1t", "q2a", "q2b", "q1s", "q2t", "q3a", "q3b", "q2s", "q3t", "q3s"]
    + [f"pick{i}" for i in range(PEER_H)] + ["decode0", "decode1", "gate"]
)
ORDER = {name: i for i, name in enumerate(PHASES)}
assert len(ORDER) == len(PHASES)

BANK_USES = [
    ("params", 0, "params_out", 1), ("keys", 1, "keys_out", 1), ("h_t0", 2, "hT", 1), ("h_t1", 3, "hT", 2),
    ("xs", 4, "xbc_in", 1), ("bc", 5, "xbc_in", 2), ("sbqk", 0, "sb_qk", 2), ("z", 1, "z_silu", 1),
    ("vq", 2, "vq_read", 1), ("kv", 3, "kv_read", 1), ("xs_t", 4, "xs_tm", 1), ("b_t", 5, "b_tm", 1),
    ("cumsum", 0, "acs", 1), ("l0", 1, "decay", 1), ("cb0", 2, "decayed", 1), ("l1", 3, "decay", 2),
    ("cb1", 4, "decayed", 2), ("y_diag", 5, "y", 1), ("y_off", 0, "y", 1), ("state", 1, "state_new", 1),
    ("sbz0", 2, "softplus", 1), ("sbz1", 3, "softplus", 2), ("sbr0", 4, "sb_w", 1), ("sbz2", 2, "softplus", 3),
    ("sbr1", 5, "sb_w", 2), ("sb_o", 0, "mixed", 2), ("sbz3", 3, "softplus", 4), ("sbr2", 4, "sb_w", 3),
    ("sbr3", 5, "sb_w", 4), ("n_t", 1, "nkT", 1), ("kcvc_t", 2, "kcvcT", 1), ("cmp", 3, "cmp_rep", 1),
    ("cmp_tt", 4, "v_bd", 1), ("cmp_kt", 5, "kbd", 1), ("cmp_s", 1, "cmp_sub", 1), ("cmp_pt", 2, "cmp_pT", 1),
    ("cmp_o", 3, "o_cmp", 1), ("s0", 4, "probs", 1), ("s1", 5, "probs", 2), ("p0", 1, "probsT", 1),
    ("s2", 4, "probs", 3), ("p1", 2, "probsT", 2), ("att_o", 0, "nsa_o", 1), ("s3", 5, "probs", 4),
    ("p2", 1, "probsT", 3), ("s4", 4, "probs", 5), ("p3", 2, "probsT", 4), ("s5", 5, "probs", 6),
    ("p4", 1, "probsT", 5), ("s6", 4, "probs", 7), ("p5", 2, "probsT", 6), ("s7", 5, "probs", 8),
    ("p6", 1, "probsT", 7), ("p7", 2, "probsT", 8), ("mix_t0", 4, "mixT", 1), ("mix_t1", 5, "mixT", 2),
    ("out0", 1, "x_mid", 1), ("out1", 2, "x_mid", 2), ("h2_t0", 3, "h2T", 1), ("h2_t1", 0, "h2T", 2),
    ("q0", 4, "q_tm", 1), ("qt0", 5, "qT", 1), ("q1", 1, "q_tm", 2), ("sc0", 2, "scores", 1), ("qt1", 3, "qT", 2),
    ("q2", 4, "q_tm", 3), ("sc1", 0, "scores", 2), ("qt2", 5, "qT", 3), ("q3", 1, "q_tm", 4), ("sc2", 2, "scores", 3),
    ("qt3", 3, "qT", 4), ("sc3", 0, "scores", 4),
]
BANK_OF = {use: n for use, n, _, _ in BANK_USES}
USE_OF = {use: [u for u, n, _, _ in BANK_USES if n == BANK_OF[use]].index(use) + 1 for use in BANK_OF}
READ_BY = {use: (by, count) for use, _, by, count in BANK_USES}


def trunk(nc, a, const_dram, x_dram, out_dram):
    fp32, u32 = mybir.dt.float32, mybir.dt.uint32
    ALU, ACT, AX = mybir.AluOpType, mybir.ActivationFunctionType, mybir.AxisListType
    V, S, T = nc.vector, nc.scalar, nc.tensor
    ctx = ExitStack()
    with ctx:
        def sb(name, shape, dt=fp32):
            return ctx.enter_context(nc.sbuf_tensor(name, shape, dt))

        width = max(hi for _, hi in CONST.values())
        consts = sb("consts", [P, width])

        def const(name):
            lo, hi = CONST[name]
            return consts[:, lo:hi]

        def const_at(name, block, n):
            lo, _ = CONST[name]
            return consts[:, bass.ds(lo + block, n)]

        ident, tri, iota16 = const("ident"), const("tri"), const("iota")
        X = sb("X", [P, BLOCKS, D])
        w_ring = sb("w_ring", [P, W_RING, KT, 512])
        u_rows = sb("u_rows", [P, U_RING, D])
        v_rows = sb("v_rows", [P, V_RING, D])
        diag = sb("diag", [P, DIAG_RING, P])
        mix = sb("mix", [P, D])
        scratch = sb("scratch", [P, D])
        hT = sb("hT", [P, KT, P])
        h2_next, h2_now = sb("h2_next", [P, D]), sb("h2_now", [P, D])
        xbcT = sb("xbcT", [P, KT, P + TAPS - 1])
        xbc = sb("xbc", [P, KT, P])
        state = sb("state", [P, SSD_W])
        sbqT, sbkT, sbv = sb("sbqT", [P, 2, P]), sb("sbkT", [P, 2, SEQ]), sb("sbv", [P, BLOCKS, 256])
        nqk = sb("nqk", [P, 7, HD])
        kcvc = sb("kcvc", [P, 2, HD])
        kk = sb("kk", [P, 2, 2, HD])
        nqT, nkT, nsv = sb("nqT", [P, 2, P]), sb("nkT", [P, 2, SEQ]), sb("nsv", [P, BLOCKS, P])
        kcvcT = sb("kcvcT", [P, SEQ + CMP_STRIDE])
        rope = sb("rope", [P, 2, 8])
        r = sb("r", [P, 4, 7, 8])
        W = [sb(f"w{i}", [P, 512]) for i in range(10)]
        b_tm = sb("b_tm", [P, 2, SSD_N])
        rows = sb("rows", [40, P])
        pos_rows = sb("pos_rows", [CMP_LEN, 2, HD])
        key_rows = sb("key_rows", [P, 2, P])
        conv_p, posT, keysT = sb("conv_p", [P, 40]), sb("posT", [P, CMP_LEN]), sb("keysT", [P, 2, P])
        n1w, catw = sb("n1w", [P, KT]), sb("catw", [P, KT])
        n2w = sb("n2w", [P, D])
        dtb, alog, dskip = sb("dtb", [P, SSD_H]), sb("alog", [P, SSD_H]), sb("dskip", [P, SSD_H])
        qkw = sb("qkw", [P, 7, HD])
        sm = {n: sb("sm_" + n, [P, c]) for n, c in dict(
            ss1=1, ms1=1, rt1=1, rs1=1, ss2=1, ms2=1, rt2=1, rs2=1, ss3=1, ms3=1, rt3=1, rs3=1, ss4=1, ms4=1, rt4=1,
            rs4=1, ss5=1, ms5=1, rt5=1, rs5=1, ssq=6, msq=6, rtq=6, rsq=6, ssc=1, msc=1, rtc=1, rsc=1,
            dtp=8, dta=8, dt=8, ea=8, dtA=8, acs=24, nacs=8, ed=24, gt=12, sg=12, mx=8, nm=8, sums=8, coef=8,
            cm=4, csum=4, crec=4, gmx=8, gsum=8, grec=8).items()}
        kn = sb("kn", [P, HD])
        k2 = sb("k2", [64, 2, HD])
        kbd = sb("kbd", [P, 64])
        sv = sb("sv", [P, 2 * PEER_H, TOPK])
        si = sb("si", [P, 2 * PEER_H, TOPK], u32)
        sif = sb("sif", [P, 2 * PEER_H, TOPK])
        cv = sb("cv", [P, PEER_H, TOPK])
        ci = sb("ci", [P, SLOTS], u32)
        ch = sb("ch", [P, 2, SLOTS], u32)
        chf = sb("chf", [P, 2, SLOTS])
        picked = sb("picked", [P, 2, SLOTS])
        idx_next, idx_now = sb("idx_next", [P, SLOTS], u32), sb("idx_now", [P, SLOTS], u32)
        g_next, g_now = sb("g_next", [P, SLOTS]), sb("g_now", [P, SLOTS])
        dots, gel, wgt = sb("dots", [P, SLOTS]), sb("gel", [P, SLOTS]), sb("wgt", [P, SLOTS])

        acc = ctx.enter_context(nc.psum_tensor("acc", [P, D], fp32))
        banks = [ctx.enter_context(nc.psum_tensor(f"bank{i}", [P, 512], fp32)) for i in range(6)]

        def bank(use):
            return banks[BANK_OF[use]]

        sems = {}

        def sig(name):
            if name not in sems:
                sems[name] = ctx.enter_context(nc.semaphore(name))
            return sems[name]

        u_in = [sig(f"u_in{i}") for i in range(U_RING)]
        v_in = [sig(f"v_in{i}") for i in range(V_RING)]
        for i in range(6):
            sig(f"bank{i}_full")
        w_in = [sig(f"w_in{i}") for i in range(W_RING)]

        def made(ins, name):
            return ins.then_inc(sig(name), 1)

        def full(ins, use):
            return ins.then_inc(sig(f"bank{BANK_OF[use]}_full"), 1)

        def wait_full(eng, use):
            eng.wait_ge(sig(f"bank{BANK_OF[use]}_full"), USE_OF[use])

        def wait_free(pe, use):
            if USE_OF[use] > 1:
                before = [u for u in BANK_OF if BANK_OF[u] == BANK_OF[use]][USE_OF[use] - 2]
                by, count = READ_BY[before]
                pe.wait_ge(sig(by), count)

        class InOrder:

            def __init__(self, eng, sem):
                self.eng, self.sem, self.n = eng, sem, 0

            def __call__(self, ins):
                self.n += 1
                ins.then_inc(self.sem, 1)
                self.eng.wait_ge(self.sem, self.n)

        CHUNKS = [("in", XS0), ("in", BC0), ("in", SBQ0), ("in", Z0), ("in", SBV0), ("kv", 0), ("cmp", 0),
                  ("out", 0), ("out", 512), ("q", 0), ("q", 512), ("q", 1024), ("q", 1536)]

        CHUNK_USES = ["xs", "bc", "sbqk", "z", "vq", "kv", "cmp", "out0", "out1", "q0", "q1", "q2", "q3"]

        def chunk(c):
            return w_ring[:, c % W_RING]

        def wait_chunk(pe, c):
            count = sum(16 * (2 if CHUNKS[k][0] in ("kv", "cmp") else 1) for k in range(c % W_RING, c + 1, W_RING))
            pe.wait_ge(w_in[c % W_RING], count)

        def mix_sync(sp, l):
            def param(dst, src):
                sp.dma_start(dst, src).then_inc(sig("params_in"), 16)

            lw = bass.ds(l, 1)

            def one(src, pattern, **k):
                return src[lw].rearrange("o " + pattern, **k)

            param(n1w[:], one(a["norm1_w"], "(p k) -> (o p) k", k=KT))
            param(rows[0:32, :], one(a["conv_w"], "t (i c) -> (o t i) c", c=P))
            param(rows[32:40, :], one(a["conv_b"], "(i c) -> (o i) c", c=P))
            param(pos_rows[:], one(a["nsa_cmp_pos"], "i j d -> (o j) i d"))
            param(key_rows[:], one(a["peer_sub_keys"], "h k d -> (o k) h d"))
            param(catw[0:64, :], one(a["ssd_norm_w"], "(p k) -> (o p) k", k=KT))
            param(catw[64:96, :], one(a["sb_out_w"], "(p k) -> (o p) k", k=KT))
            param(catw[96:128, :], one(a["nsa_out_w"], "(p k) -> (o p) k", k=KT))
            for dst, src in ((n2w, "norm2_w"), (dtb, "dt_bias"), (alog, "a_log"), (dskip, "d_skip")):
                param(dst[:], a[src][lw].to_broadcast([P, dst.shape[1]]))
            param(qkw[:, 0:3, :], one(a["nsa_k_norm_w"], "r d -> o (r d)").to_broadcast([P, 3 * HD]))
            for h in range(NSA_H):
                param(qkw[:, 3 + h, :], a["nsa_q_norm_w"][lw].to_broadcast([P, HD]))
            for c, (what, c0) in enumerate(CHUNKS):
                if c >= W_RING:
                    wait_full(sp, CHUNK_USES[c - W_RING])
                dst = chunk(c)
                done = w_in[c % W_RING]
                if what == "in":
                    sp.dma_start(dst, one(a["w_in"], "(p k) n -> (o p) k n", k=KT)[:, :, c0:c0 + 512]).then_inc(done, 16)
                elif what == "kv":
                    wi = one(a["w_in"], "(p k) n -> (o p) k n", k=KT)
                    sp.dma_start(dst[:, :, 0:8], wi[:, :, DT0:DT0 + 8]).then_inc(done, 16)
                    sp.dma_start(dst[:, :, 8:8 + KVW], wi[:, :, KV0:IN_DIM]).then_inc(done, 16)
                elif what == "cmp":
                    flat = dst.rearrange("p k n -> p (k n)")[:, 0:CMP_LEN * HD].rearrange("p (j e) -> p j e", e=HD)
                    for i in range(2):
                        sp.dma_start(flat[64 * i:64 * i + 64],
                                     a["nsa_cmp_w"][lw, i].rearrange("o (j d) e -> (o d) j e", d=HD)).then_inc(done, 16)
                elif what == "out":
                    sp.dma_start(dst, one(a["w_out"], "(p k) n -> (o p) k n", k=KT)[:, :, c0:c0 + 512]).then_inc(done, 16)
                else:
                    sp.dma_start(dst, one(a["peer_w_q"], "(p k) n -> (o p) k n", k=KT)[:, :, c0:c0 + 512]).then_inc(done, 16)

        PARAMS = 12 + 1 + NSA_H

        def mix_tensor(pe, b):
            def transposes(use, tiles, n=P):
                for i, tile in enumerate(tiles):
                    last = T.transpose(bank(use)[:, i * n:(i + 1) * n], tile, ident)
                return full(last, use)

            def h_transposed(src, names, ready, phase):
                pe.wait_ge(sig(ready), 1)
                v = src[:].rearrange("p (f k) -> p k f", k=KT)
                for half, use in enumerate(names):
                    wait_free(pe, use)
                    transposes(use, [v[:, 4 * half + i] for i in range(4)])

            def features(use, c, lo, hi):
                if lo == 0:
                    wait_free(pe, use)
                    wait_chunk(pe, c)
                for m in range(lo, hi):
                    for k in range(KT):
                        last = T.matmul(bank(use)[:, m * P:(m + 1) * P], chunk(c)[:, k, m * P:(m + 1) * P], hT[:, k, :],
                                        start=(k == 0), stop=(k == KT - 1))
                if hi == 4:
                    full(last, use)

            def tokens(use, c, lo, hi, n=512):
                if lo == 0:
                    wait_free(pe, use)
                    wait_chunk(pe, c)
                for k in range(lo, hi):
                    last = T.matmul(bank(use)[:, 0:n], hT[:, k, :], chunk(c)[:, k, 0:n], start=(k == 0), stop=(k == KT - 1))
                if hi == KT:
                    full(last, use)

            yield "params"
            pe.wait_ge(sig("params_in"), 16 * PARAMS)
            T.transpose(bank("params")[:, 0:40], rows[:], ident[0:40, 0:40])
            full(T.transpose(bank("params")[:, 64:96], pos_rows[:].rearrange("j i d -> j (i d)"), ident[0:32, 0:32]), "params")
            transposes("keys", [key_rows[:, i] for i in range(2)])
            yield "norm1_t"
            h_transposed(mix, ("h_t0", "h_t1"), "normed1", 0)
            yield "xs0"
            pe.wait_ge(sig("hT"), 2)
            features("xs", 0, 0, 2)
            yield "xs1"
            features("xs", 0, 2, 4)
            yield "bc0"
            features("bc", 1, 0, 2)
            yield "bc1"
            features("bc", 1, 2, 4)
            yield "sbqk0"
            features("sbqk", 2, 0, 2)
            yield "sbqk1"
            features("sbqk", 2, 2, 4)
            yield "z0"
            tokens("z", 3, 0, 4)
            yield "z1"
            tokens("z", 3, 4, 8)
            yield "vq0"
            tokens("vq", 4, 0, 4)
            yield "vq1"
            tokens("vq", 4, 4, 8)
            yield "kv0"
            tokens("kv", 5, 0, 4, 8 + KVW)
            yield "kv1"
            tokens("kv", 5, 4, 8, 8 + KVW)
            yield "xs_t"
            pe.wait_ge(sig("xbc"), 1)
            wait_free(pe, "xs_t")
            transposes("xs_t", [xbc[:, i] for i in range(4)])
            wait_free(pe, "b_t")
            transposes("b_t", [xbc[:, 4 + g] for g in range(2)])
            yield "cumsum"
            pe.wait_ge(sig("dtA"), 1)
            wait_free(pe, "cumsum")
            T.matmul(bank("cumsum")[:, 0:8], tri, sm["dtA"][:], start=True, stop=True)
            full(T.matmul(bank("cumsum")[:, 8:16], const("ones"), sm["dtA"][:], start=True, stop=True), "cumsum")
            for g in range(2):
                yield f"decay{g}"
                use = f"l{g}"
                wait_free(pe, use)
                out = bank(use)[:].rearrange("p (h l) -> p h l", h=4)
                T.matmul(out, ident, const("later").unsqueeze(1).to_broadcast([P, 4, P]), start=True, stop=False)
                for h in range(4):
                    last = T.matmul(out[:, h], sm["dtA"][:, 4 * g + h:4 * g + h + 1].to_broadcast([P, P]), tri,
                                    start=False, stop=(h == 3))
                full(last, use)
                wait_free(pe, f"cb{g}")
                full(T.matmul(bank(f"cb{g}")[:, 0:P], xbc[:, 4 + g], xbc[:, 6 + g], start=True, stop=True), f"cb{g}")
            yield "y_diag"
            wait_free(pe, "y_diag")
            for g in range(2):
                pe.wait_ge(sig("decayed"), g + 1)
                pe.wait_ge(sig("x_dec"), 1)
                for h in range(4):
                    last = T.matmul(bank("y_diag")[:, (4 * g + h) * HD:(4 * g + h + 1) * HD],
                                    W[4 + g][:, h * P:(h + 1) * P], W[2][:, (4 * g + h) * HD:(4 * g + h + 1) * HD],
                                    start=True, stop=True)
            full(last, "y_diag")
            yield "y_off"
            wait_free(pe, "y_off")
            pe.wait_ge(sig("state_kept"), 1)
            for g in range(2):
                last = T.matmul(bank("y_off")[:, 256 * g:256 * g + 256], xbc[:, 6 + g], state[:, 256 * g:256 * g + 256],
                                start=True, stop=True)
            full(last, "y_off")
            wait_free(pe, "state")
            pe.wait_ge(sig("b_tm"), 1)
            for g in range(2):
                last = T.matmul(bank("state")[:, 256 * g:256 * g + 256], b_tm[:, g], W[3][:, 256 * g:256 * g + 256],
                                start=True, stop=True)
            full(last, "state")

            def sb_scores(use, h, start):
                base, hp = 64 * (h % 2), h // 2
                for kb in range(BLOCKS):
                    last = T.matmul(bank(use)[:, kb * P:(kb + 1) * P], sbkT[base:base + 64, hp, kb * P:(kb + 1) * P],
                                    sbqT[base:base + 64, hp, :], start=start, stop=start)
                return last

            for i in range(SB_H + 2):
                yield f"sb{i}"
                if i < SB_H:
                    if i == 0:
                        pe.wait_ge(sig("sb_qk"), 2)
                    wait_free(pe, f"sbz{i}")
                    full(sb_scores(f"sbz{i}", i, True), f"sbz{i}")
                if 1 <= i <= SB_H:
                    h, use = i - 1, f"sbr{i - 1}"
                    wait_free(pe, use)
                    T.matmul(bank(use)[:], ident, const_at("stay_neg", (BLOCKS - 1 - b) * P, SEQ), start=True, stop=False)
                    sb_scores(use, h, False)
                    pe.wait_ge(sig("softplus"), h + 1)
                    sp_t = W[4 + h % 2]
                    T.matmul(bank(use)[:], const("neg_tri_ge"), sp_t[:], start=False, stop=False)
                    for kb in range(1, BLOCKS):
                        last = T.matmul(bank(use)[:, 0:kb * P].rearrange("p (k q) -> p k q", k=kb), const("neg_ones"),
                                        sp_t[:, kb * P:(kb + 1) * P].unsqueeze(1).to_broadcast([P, kb, P]),
                                        start=False, stop=(kb == BLOCKS - 1))
                    full(last, use)
                if i >= 2:
                    h = i - 2
                    if h == 0:
                        wait_free(pe, "sb_o")
                        pe.wait_ge(sig("sb_v"), 1)
                    pe.wait_ge(sig("sb_w"), h + 1)
                    for kb in range(BLOCKS):
                        last = T.matmul(bank("sb_o")[:, h * HD:(h + 1) * HD], W[7 + h % 2][:, kb * P:(kb + 1) * P],
                                        sbv[:, kb, h * HD:(h + 1) * HD], start=(kb == 0), stop=(kb == BLOCKS - 1))
                    if h == SB_H - 1:
                        full(last, "sb_o")
                    else:
                        made(last, "sb_head")

            yield "nsa_t"
            pe.wait_ge(sig("roped"), 1)
            wait_free(pe, "n_t")
            q2 = nqk[:, 3:7, :].rearrange("p h d -> p (h d)")
            transposes("n_t", [q2[:, 0:P], q2[:, P:2 * P], kk[:, 0].rearrange("p a d -> p (a d)"),
                               kk[:, 1].rearrange("p a d -> p (a d)")])
            wait_free(pe, "kcvc_t")
            transposes("kcvc_t", [kcvc[:].rearrange("p a d -> p (a d)")])
            cmp_w = chunk(6).rearrange("p k n -> p (k n)")[:, 0:CMP_LEN * HD].rearrange("p (j e) -> p j e", e=HD)
            for i in range(8):
                yield f"cmp{i}"
                if i == 0:
                    pe.wait_ge(sig("kcvcT"), 1)
                    wait_chunk(pe, 6)
                    wait_free(pe, "cmp")
                if i == 4:
                    pe.wait_ge(sig("cmp_keys"), 1)
                kv, part = i // 4, i % 4
                lo, hi = 64 * kv, 64 * kv + 64
                for j in range(8 * part, 8 * part + 8):
                    at = bank("cmp")[0:64, CMP_PAD * kv:CMP_PAD * (kv + 1)]
                    T.matmul(at, cmp_w[lo:hi, j, :], kcvcT[lo:hi, j:j + (CMP_PAD - 1) * CMP_STRIDE + 1:CMP_STRIDE],
                             start=(j == 0), stop=False)
                    last = T.matmul(at, cmp_w[lo:hi, j, :], posT[lo:hi, j:j + 1].to_broadcast([64, CMP_PAD]),
                                    start=False, stop=(j == CMP_LEN - 1))
                if i == 3:
                    made(last, "cmp_keys")
                if i == 7:
                    full(last, "cmp")
            yield "cmp_t"
            wait_free(pe, "cmp_tt")
            pe.wait_ge(sig("cmp_rep"), 1)
            for kv in range(2):
                last = T.transpose(bank("cmp_tt")[:, kv * HD:(kv + 1) * HD], W[6][0:64, kv * P:(kv + 1) * P], ident[0:64, 0:64])
            full(last, "cmp_tt")
            yield "cmp_kt"
            wait_free(pe, "cmp_kt")
            pe.wait_ge(sig("k2"), 1)
            full(T.transpose(bank("cmp_kt")[:, 0:64], k2[:].rearrange("p a d -> p (a d)"), ident[0:64, 0:64]), "cmp_kt")
            yield "cmp_s"
            wait_free(pe, "cmp_s")
            pe.wait_ge(sig("kbd"), 1)
            T.matmul(bank("cmp_s")[:, 0:P], ident, const_at("cmp_neg", b * P, P), start=True, stop=False)
            for hp in range(2):
                last = T.matmul(bank("cmp_s")[:, 64 * hp:64 * hp + 64], nqT[:, hp], kbd[:], start=False, stop=(hp == 1))
            full(last, "cmp_s")
            yield "cmp_pt"
            wait_free(pe, "cmp_pt")
            pe.wait_ge(sig("cmp_p"), 1)
            transposes("cmp_pt", [W[7][:, 0:P]])
            yield "cmp_o"
            wait_free(pe, "cmp_o")
            pe.wait_ge(sig("cmp_pT"), 1)
            full(T.matmul(bank("cmp_o")[:, 0:256], W[8][:, 0:P], W[9][:, 0:256], start=True, stop=True), "cmp_o")

            units = 2 * NSA_H
            for i in range(units + 2):
                yield f"att{i}"
                if i < units:
                    br, h = i // NSA_H, i % NSA_H
                    base, use = 64 * (h % 2), f"s{i}"
                    wait_free(pe, use)
                    T.matmul(bank(use)[:], ident, const_at("causal_neg", (BLOCKS - 1 - b) * P, SEQ), start=True, stop=False)
                    full(T.matmul(bank(use)[:], nqT[base:base + 64, h // 2], nkT[base:base + 64, br], start=False, stop=True), use)
                if 1 <= i <= units:
                    use = f"p{i - 1}"
                    wait_free(pe, use)
                    pe.wait_ge(sig("probs"), i)
                    transposes(use, [W[2 + (i - 1) % 2][:, kb * P:(kb + 1) * P] for kb in range(BLOCKS)])
                if i >= 2:
                    j = i - 2
                    br, h = j // NSA_H, j % NSA_H
                    if j == 0:
                        wait_free(pe, "att_o")
                    pe.wait_ge(sig("probsT"), j + 1)
                    for kb in range(BLOCKS):
                        last = T.matmul(bank("att_o")[:, j * HD:(j + 1) * HD], W[4 + j % 2][:, kb * P:(kb + 1) * P],
                                        nsv[:, kb, br * HD:(br + 1) * HD], start=(kb == 0), stop=(kb == BLOCKS - 1))
                    if j == units - 1:
                        full(last, "att_o")
                    else:
                        made(last, "att_head")
            yield "mix_t"
            pe.wait_ge(sig("mixed"), 3)
            h_transposed(mix, ("mix_t0", "mix_t1"), "mixed", 0)
            for i in range(4):
                yield f"out{i}"
                if i == 0:
                    pe.wait_ge(sig("mixT"), 2)
                tokens(f"out{i // 2}", 7 + i // 2, 4 * (i % 2), 4 * (i % 2) + 4)
            yield "norm2_t"
            h_transposed(h2_next, ("h2_t0", "h2_t1"), "normed2", 0)

            def q_part(c, half):
                if c == 0 and half == 0:
                    pe.wait_ge(sig("h2T"), 2)
                tokens(f"q{c}", 9 + c, 4 * half, 4 * half + 4)

            def q_turned(c):
                wait_free(pe, f"qt{c}")
                pe.wait_ge(sig("q_tm"), c + 1)
                transposes(f"qt{c}", [W[6][:, i * P:(i + 1) * P] for i in range(4)])

            def q_scores(c):
                wait_free(pe, f"sc{c}")
                pe.wait_ge(sig("qT"), c + 1)
                for i in range(4):
                    last = T.matmul(bank(f"sc{c}")[:, i * P:(i + 1) * P], W[8][:, i * P:(i + 1) * P], keysT[:, i % 2],
                                    start=True, stop=True)
                full(last, f"sc{c}")

            for c in range(4):
                yield f"q{c}a"
                q_part(c, 0)
                yield f"q{c}b"
                q_part(c, 1)
                if c >= 1:
                    yield f"q{c - 1}s"
                    q_scores(c - 1)
                yield f"q{c}t"
                q_turned(c)
            yield "q3s"
            q_scores(3)

        def mix_scalar(act, b, chain):
            def copy(dst, src, **k):
                return S.activation(dst, src, ACT.Copy, **k)

            def root(n):
                act.wait_ge(sig("mean" + n), 1)
                made(S.activation(sm["rt" + n][:], sm["ms" + n][:], ACT.Sqrt), "root" + n)

            def squares(n, src, width):
                S.activation(scratch[:, 0:width], src, ACT.Square, accum_out=sm["ss" + n][:]).then_inc(sig("squares" + n), 1)
                act.wait_ge(sig("squares" + n), 1)

            yield "params"
            wait_full(act, "params")
            chain(copy(conv_p[:], bank("params")[:, 0:40]))
            made(copy(posT[:], bank("params")[:, 64:96]), "params_out")
            wait_full(act, "keys")
            made(copy(keysT[:].rearrange("p a d -> p (a d)"), bank("keys")[:, 0:256]), "keys_out")
            yield "norm1"
            squares("1", X[:, bass.ds(b, 1), :].rearrange("p o d -> p (o d)"), D)
            root("1")
            yield "xs1"
            wait_full(act, "xs")
            made(copy(xbcT[:, 0:4, TAPS - 1:], bank("xs")[:].rearrange("p (i t) -> p i t", i=4)), "xbc_in")
            yield "bc1"
            wait_full(act, "bc")
            made(copy(xbcT[:, 4:8, TAPS - 1:], bank("bc")[:].rearrange("p (i t) -> p i t", i=4)), "xbc_in")
            yield "sbqk1"
            wait_full(act, "sbqk")
            made(copy(sbqT[:].rearrange("p a q -> p (a q)"), bank("sbqk")[:, 0:256], scale=SCALE), "sb_qk")
            made(copy(sbkT[:, :, bass.ds(b * P, P)], bank("sbqk")[:, 256:512].rearrange("p (a q) -> p a q", a=2)), "sb_qk")
            yield "z1"
            wait_full(act, "z")
            made(S.activation(W[0][:], bank("z")[:], ACT.Silu), "z_silu")
            yield "conv_out"
            act.wait_ge(sig("conv"), 8 * TAPS)
            made(S.activation(xbc[:].rearrange("p i t -> p (i t)"), scratch[:], ACT.Silu), "xbc")
            yield "xs_t"
            wait_full(act, "xs_t")
            made(copy(W[1][:], bank("xs_t")[:]), "xs_tm")
            wait_full(act, "b_t")
            made(copy(b_tm[:].rearrange("p g n -> p (g n)"), bank("b_t")[:, 0:256]), "b_tm")
            yield "dt"
            act.wait_ge(sig("kv_read"), 1)
            chain(S.activation(sm["dta"][:], sm["dtp"][:], ACT.Abs))
            chain(S.activation(sm["dta"][:], sm["dta"][:], ACT.Exp, scale=-1.0))
            chain(S.activation(sm["dta"][:], sm["dta"][:], ACT.Ln, bias=1.0))
            made(S.activation(sm["ea"][:], alog[:], ACT.Exp), "dt_log")
            chain(S.activation(sm["sg"][:], sm["gt"][:], ACT.Exp, scale=-1.0))
            act.wait_ge(sig("dt_log"), 1)
            yield "cumsum"
            act.wait_ge(sig("acs"), 1)
            made(S.activation(sm["ed"][:], sm["acs"][:], ACT.Exp), "ed")
            for g in range(2):
                yield f"decay{g}"
                wait_full(act, f"l{g}")
                for h in range(4):
                    last = S.activation(W[4 + g][:, h * P:(h + 1) * P], bank(f"l{g}")[:, h * P:(h + 1) * P], ACT.Exp,
                                        bias=sm["nacs"][:, 4 * g + h:4 * g + h + 1])
                    if h < 3:
                        made(last, "decay_head")
                made(last, "decay")
            yield "y_sum"
            act.wait_ge(sig("y"), 1)
            squares("2", W[6][:], SSD_W)
            root("2")
            for i in range(SB_H + 2):
                yield f"sb{i}"
                if i < SB_H:
                    wait_full(act, f"sbz{i}")
                    if i:
                        act.wait_ge(sig("softplus"), i)
                    chain(S.activation(W[2][:], bank(f"sbz{i}")[:], ACT.Abs))
                    chain(S.activation(W[2][:], W[2][:], ACT.Exp, scale=-1.0))
                    made(S.activation(W[2][:], W[2][:], ACT.Ln, bias=1.0), "sb_log")
                if 1 <= i <= SB_H:
                    h = i - 1
                    wait_full(act, f"sbr{h}")
                    if h >= 2:
                        act.wait_ge(sig("sb_head"), h - 1)
                    made(S.activation(W[7 + h % 2][:], bank(f"sbr{h}")[:], ACT.Exp), "sb_w")
            yield "sb_norm"
            wait_full(act, "sb_o")
            squares("3", bank("sb_o")[:, 0:256], 256)
            root("3")
            yield "nsa_norm"
            root("q")
            yield "nsa_t"
            wait_full(act, "n_t")
            made(copy(nqT[:].rearrange("p a q -> p (a q)"), bank("n_t")[:, 0:256]), "nqT")
            yield "cmp_norm"
            root("c")
            yield "cmp_kt"
            wait_full(act, "cmp_kt")
            made(copy(kbd[:], bank("cmp_kt")[:, 0:64]), "kbd")
            yield "cmp_s"
            act.wait_ge(sig("cmp_sub"), 1)
            made(S.activation(W[7][:, 0:P], W[7][:, 0:P], ACT.Exp, scale=SCALE), "cmp_e")
            yield "cmp_pt"
            wait_full(act, "cmp_pt")
            made(copy(W[8][:, 0:P], bank("cmp_pt")[:, 0:P]), "cmp_pT")
            for i in range(2 * NSA_H):
                yield f"att{i}"
                act.wait_ge(sig("row_max"), i + 1)
                if i >= 2:
                    wait_full(act, f"p{i - 2}")
                made(S.activation(W[2 + i % 2][:], bank(f"s{i}")[:], ACT.Exp, bias=sm["nm"][:, i:i + 1], scale=SCALE,
                                  accum_out=sm["sums"][:, i:i + 1]), "probs")
            yield "nsa_sum"
            act.wait_ge(sig("nsa_o"), 1)
            squares("4", W[0][:, 0:256], 256)
            root("4")
            yield "norm2"
            act.wait_ge(sig("x_mid"), 2)
            squares("5", X[:, bass.ds(b, 1), :].rearrange("p o d -> p (o d)"), D)
            root("5")
            yield "norm2_t"
            for half in range(2):
                wait_full(act, f"h2_t{half}")
                made(copy(hT[:, 4 * half:4 * half + 4].rearrange("p k t -> p (k t)"), bank(f"h2_t{half}")[:]), "h2T")
            for c in range(4):
                yield f"q{c}b"
                wait_full(act, f"q{c}")
                if c:
                    wait_full(act, f"qt{c - 1}")
                made(copy(W[6][:], bank(f"q{c}")[:]), "q_tm")
                if c >= 1:
                    yield f"q{c - 1}s"
                    wait_full(act, f"sc{c - 1}")
                    if c >= 2:
                        act.wait_ge(sig("top_keys"), c - 1)
                    made(copy(W[0][:], bank(f"sc{c - 1}")[:]), "scores")
                yield f"q{c}t"
                wait_full(act, f"qt{c}")
                made(copy(W[8][:], bank(f"qt{c}")[:]), "qT")
            yield "q3s"
            wait_full(act, "sc3")
            act.wait_ge(sig("top_keys"), 3)
            made(copy(W[0][:], bank("sc3")[:]), "scores")
            yield "gate"
            act.wait_ge(sig("g_sub"), 1)
            made(S.activation(g_next[:], g_next[:], ACT.Exp), "g_exp")

        def mix_vector(dve, b, step, chain):
            def tt(out, in0, in1, op=ALU.mult):
                return V.tensor_tensor(out, in0, in1, op)

            def over(scalars, n):
                return scalars.unsqueeze(2).to_broadcast([P, scalars.shape[1], n])

            def mean(n, width):
                dve.wait_ge(sig("squares" + n), 1)
                made(V.tensor_scalar(sm["ms" + n][:], sm["ss" + n][:], 1.0 / width, EPS, ALU.mult, ALU.add), "mean" + n)

            def rstd(n):
                dve.wait_ge(sig("root" + n), 1)
                chain(V.reciprocal(sm["rs" + n][:], sm["rt" + n][:]))

            Xb = X[:, bass.ds(b, 1), :].rearrange("p o d -> p (o d)")
            yield "norm1"
            carry = const_at("carry", step, 1)
            made(V.tensor_scalar(state[:], state[:], carry, None, ALU.mult), "state_kept")
            chain(V.tensor_scalar(xbcT[:, :, 0:TAPS - 1], xbcT[:, :, 0:TAPS - 1], carry, None, ALU.mult))
            chain(V.tensor_copy(rope[:].rearrange("p a d -> p (a d)"), const_at("rope", b * 16, 16)))
            mean("1", D)
            rstd("1")
            made(V.tensor_scalar(mix[:], Xb, sm["rs1"][:], None, ALU.mult), "normed1")
            yield "norm1_t"
            for half in range(2):
                use = f"h_t{half}"
                wait_full(dve, use)
                dve.wait_ge(sig("params_in"), 16 * PARAMS)
                made(tt(hT[:, 4 * half:4 * half + 4], bank(use)[:].rearrange("p (k t) -> p k t", k=4),
                        over(n1w[:, 4 * half:4 * half + 4], P)), "hT")
            acc_v = scratch[:].rearrange("p (i t) -> p i t", i=8)
            for t in range(TAPS):
                yield f"conv{t}"
                if t == 0:
                    dve.wait_ge(sig("xbc_in"), 2)
                    dve.wait_ge(sig("params_out"), 1)
                for i in range(8):
                    tap = conv_p[:, t * 8 + i:t * 8 + i + 1]
                    if t == 0:
                        ins = V.tensor_scalar(acc_v[:, i], xbcT[:, i, 0:P], tap, conv_p[:, 32 + i:33 + i], ALU.mult, ALU.add)
                    else:
                        dve.wait_ge(sig("conv"), 8 * (t - 1) + i + 1)
                        ins = V.scalar_tensor_tensor(acc_v[:, i], xbcT[:, i, t:t + P], tap, acc_v[:, i], ALU.mult, ALU.add)
                    made(ins, "conv")
            yield "conv_out"
            dve.wait_ge(sig("conv"), 8 * TAPS)
            chain(V.tensor_copy(xbcT[:, :, 0:TAPS - 1], xbcT[:, :, P:P + TAPS - 1]))
            yield "vq1"
            wait_full(dve, "vq")
            made(V.tensor_copy(sbv[:, bass.ds(b, 1), :].rearrange("p o d -> p (o d)"), bank("vq")[:, 0:256]), "sb_v")
            made(V.tensor_copy(nqk[:, 3:7, :].rearrange("p h d -> p (h d)"), bank("vq")[:, 256:512]), "vq_read")
            yield "kv1"
            wait_full(dve, "kv")
            pairs = bank("kv")[:, 8:8 + 6 * HD].rearrange("p (i a d) -> p i a d", a=2, d=HD)
            chain(V.tensor_copy(nqk[:, 0:3, :], pairs[:, :, 0]))
            chain(V.tensor_copy(kcvc[:, 1], pairs[:, 0, 1]))
            chain(V.tensor_copy(nsv[:, bass.ds(b, 1), :].rearrange("p o (a d) -> p (o a) d", a=2), pairs[:, 1:3, 1]))
            chain(V.tensor_copy(sm["gt"][:], bank("kv")[:, 8 + 6 * HD:8 + KVW]))
            made(tt(sm["dtp"][:], bank("kv")[:, 0:8], dtb[:], ALU.add), "kv_read")
            yield "dt"
            dve.wait_ge(sig("dt_log"), 1)
            chain(V.scalar_tensor_tensor(sm["dt"][:], sm["dtp"][:], 0.0, sm["dta"][:], ALU.max, ALU.add))
            made(V.scalar_tensor_tensor(sm["dtA"][:], sm["dt"][:], -1.0, sm["ea"][:], ALU.mult, ALU.mult), "dtA")
            yield "cumsum"
            wait_full(dve, "cumsum")
            chain(V.tensor_copy(sm["acs"][:, 0:16], bank("cumsum")[:, 0:16]))
            chain(V.tensor_scalar(sm["nacs"][:], sm["acs"][:, 0:8], -1.0, None, ALU.mult))
            made(tt(sm["acs"][:, 16:24], sm["acs"][:, 8:16], sm["acs"][:, 0:8], ALU.subtract), "acs")
            dve.wait_ge(sig("xs_tm"), 1)
            xs_tm = W[1][:].rearrange("p (h d) -> p h d", d=HD)
            x_dt, x_dec = (W[n][:].rearrange("p (h d) -> p h d", d=HD) for n in (2, 3))
            chain(tt(x_dt, xs_tm, over(sm["dt"][:], HD)))
            dve.wait_ge(sig("ed"), 1)
            made(tt(x_dec, x_dt, over(sm["ed"][:, 16:24], HD)), "x_dec")
            for g in range(2):
                yield f"decay{g}"
                dve.wait_ge(sig("decay"), g + 1)
                wait_full(dve, f"cb{g}")
                m = W[4 + g][:].rearrange("p (h l) -> p h l", h=4)
                made(tt(m, m, bank(f"cb{g}")[:, 0:P].unsqueeze(1).to_broadcast([P, 4, P])), "decayed")
            yield "y_sum"
            y = W[6][:].rearrange("p (h d) -> p h d", d=HD)
            wait_full(dve, "y_off")
            chain(tt(y, bank("y_off")[:].rearrange("p (h d) -> p h d", d=HD), over(sm["ed"][:, 0:8], HD)))
            wait_full(dve, "y_diag")
            chain(tt(W[6][:], bank("y_diag")[:], W[6][:], ALU.add))
            chain(tt(W[7][:].rearrange("p (h d) -> p h d", d=HD), xs_tm, over(dskip[:], HD)))
            chain(tt(W[6][:], W[6][:], W[7][:], ALU.add))
            dve.wait_ge(sig("z_silu"), 1)
            made(tt(W[6][:], W[6][:], W[0][:]), "y")
            wait_full(dve, "state")
            s3 = state[:].rearrange("p (h d) -> p h d", d=HD)
            chain(tt(s3, s3, over(sm["ed"][:, 8:16], HD)))
            made(tt(state[:], bank("state")[:], state[:], ALU.add), "state_new")
            mean("2", SSD_W)
            rstd("2")
            made(V.tensor_scalar(mix[:, 0:SSD_W], W[6][:], sm["rs2"][:], None, ALU.mult), "mixed")
            for i in range(SB_H):
                yield f"sb{i}"
                dve.wait_ge(sig("sb_log"), i + 1)
                if i >= 2:
                    wait_full(dve, f"sbr{i - 2}")
                sp_t = W[4 + i % 2]
                ins = V.scalar_tensor_tensor(sp_t[:], bank(f"sbz{i}")[:], 0.0, W[2][:], ALU.max, ALU.add)
                chain(ins)
                made(tt(sp_t[:], sp_t[:], const_at("stay", (BLOCKS - 1 - b) * P, SEQ)), "softplus")
            yield "sb_norm"
            mean("3", 256)
            rstd("3")
            made(V.tensor_scalar(mix[:, SSD_W:SSD_W + 256], bank("sb_o")[:, 0:256], sm["rs3"][:], None, ALU.mult), "mixed")
            yield "nsa_norm"
            sq = W[9][:, 0:384].rearrange("p (h d) -> p h d", d=HD)
            chain(tt(sq, nqk[:, 1:7], nqk[:, 1:7]))
            V.tensor_reduce(sm["ssq"][:], sq, AX.X, ALU.add).then_inc(sig("squaresq"), 1)
            mean("q", HD)
            rstd("q")
            chain(tt(nqk[:, 1:7], nqk[:, 1:7], over(sm["rsq"][:], HD)))
            chain(tt(nqk[:, 1:7], nqk[:, 1:7], qkw[:, 1:7]))
            chain(V.tensor_scalar(sm["sg"][:], sm["sg"][:], 1.0, None, ALU.add))
            chain(V.reciprocal(sm["sg"][:], sm["sg"][:]))
            yield "nsa_rope"
            x1, x2 = nqk[:, :, 0:8], nqk[:, :, 8:16]
            cos, sin = (rope[:, i, :].unsqueeze(1).to_broadcast([P, 7, 8]) for i in range(2))
            chain(tt(r[:, 0], x1, cos))
            chain(tt(r[:, 1], x2, sin))
            chain(tt(r[:, 2], x2, cos))
            chain(tt(r[:, 3], x1, sin))
            chain(tt(x1, r[:, 0], r[:, 1], ALU.subtract))
            chain(tt(x2, r[:, 2], r[:, 3], ALU.add))
            chain(V.tensor_copy(kcvc[:, 0], nqk[:, 0]))
            chain(V.tensor_copy(kk[:, :, 0], nqk[:, 1:3]))
            made(V.tensor_copy(kk[:, :, 1], nqk[:, 1:3]), "roped")
            yield "nsa_t"
            dve.wait_ge(sig("nqT"), 1)
            wait_full(dve, "n_t")
            made(V.tensor_copy(nkT[:, :, bass.ds(b * P, P)], bank("n_t")[:, 256:512].rearrange("p (a t) -> p a t", a=2)), "nkT")
            wait_full(dve, "kcvc_t")
            made(V.tensor_copy(kcvcT[:, bass.ds(b * P, P)], bank("kcvc_t")[:, 0:P]), "kcvcT")
            yield "cmp_t"
            wait_full(dve, "cmp")
            made(V.tensor_copy(W[6][0:64, 0:256].rearrange("p (v a c) -> p v a c", v=2, a=4),
                               bank("cmp")[0:64, 0:64].rearrange("p (v c) -> p v c", v=2).unsqueeze(2).to_broadcast([64, 2, 4, 32])),
                 "cmp_rep")
            yield "cmp_norm"
            wait_full(dve, "cmp_tt")
            tt_bank = bank("cmp_tt")
            chain(V.tensor_copy(kn[:], tt_bank[:, 0:HD]))
            chain(tt(W[9][:, 256:320], kn[:], kn[:]))
            V.tensor_reduce(sm["ssc"][:], W[9][:, 256:320], AX.X, ALU.add).then_inc(sig("squaresc"), 1)
            mean("c", HD)
            head_of = const("head_of")
            made(tt(W[9][:, 0:256].rearrange("p (h d) -> p h d", d=HD), tt_bank[:, HD:2 * HD].unsqueeze(1).to_broadcast([P, 4, HD]),
                    over(head_of, HD)), "v_bd")
            rstd("c")
            chain(V.tensor_scalar(kn[:], kn[:], sm["rsc"][:], None, ALU.mult))
            chain(tt(kn[:], kn[:], qkw[:, 0]))
            made(tt(k2[:], kn[0:64].unsqueeze(1).to_broadcast([64, 2, HD]),
                    head_of[0:64, 0:2].unsqueeze(2).to_broadcast([64, 2, HD])), "k2")
            yield "cmp_s"
            wait_full(dve, "cmp_s")
            sc = bank("cmp_s")[:, 0:P].rearrange("p (h c) -> p h c", h=4)
            pc = W[7][:, 0:P].rearrange("p (h c) -> p h c", h=4)
            chain(V.tensor_reduce(sm["cm"][:], sc, AX.X, ALU.max))
            made(tt(pc, sc, over(sm["cm"][:], CMP_PAD), ALU.subtract), "cmp_sub")
            dve.wait_ge(sig("cmp_e"), 1)
            chain(V.tensor_reduce(sm["csum"][:], pc[:, :, 0:CMP_PAD - 1], AX.X, ALU.add))
            chain(V.reciprocal(sm["crec"][:], sm["csum"][:]))
            chain(tt(pc, pc, over(sm["crec"][:], CMP_PAD)))
            made(tt(W[7][:, 0:P], W[7][:, 0:P], const_at("cmp_seen", b * P, P)), "cmp_p")
            yield "cmp_o"
            wait_full(dve, "cmp_o")
            o = W[0][:, 0:256].rearrange("p (h d) -> p h d", d=HD)
            gates = sm["sg"][:].rearrange("p (h b) -> p b h", b=3)
            made(tt(o, bank("cmp_o")[:, 0:256].rearrange("p (h d) -> p h d", d=HD), over(gates[:, 0], HD)), "o_cmp")
            for i in range(2 * NSA_H + 1):
                yield f"att{i}"
                if i < 2 * NSA_H:
                    wait_full(dve, f"s{i}")
                    chain(V.reduce_max(sm["mx"][:, i:i + 1], bank(f"s{i}")[:], AX.X))
                    made(V.tensor_scalar(sm["nm"][:, i:i + 1], sm["mx"][:, i:i + 1], -SCALE, None, ALU.mult), "row_max")
                if i >= 1:
                    wait_full(dve, f"p{i - 1}")
                    if i >= 3:
                        dve.wait_ge(sig("att_head"), i - 2)
                    made(V.tensor_copy(W[4 + (i - 1) % 2][:], bank(f"p{i - 1}")[:]), "probsT")
            yield "nsa_sum"
            chain(V.reciprocal(sm["coef"][:], sm["sums"][:]))
            cf = sm["coef"][:].rearrange("p (b h) -> p b h", b=2)
            chain(tt(cf, cf, gates[:, 1:3]))
            wait_full(dve, "att_o")
            t8 = W[1][:].rearrange("p (h d) -> p h d", d=HD)
            chain(tt(t8, bank("att_o")[:].rearrange("p (h d) -> p h d", d=HD), over(sm["coef"][:], HD)))
            chain(tt(W[0][:, 0:256], W[0][:, 0:256], W[1][:, 0:256], ALU.add))
            made(tt(W[0][:, 0:256], W[0][:, 0:256], W[1][:, 256:512], ALU.add), "nsa_o")
            mean("4", 256)
            rstd("4")
            made(V.tensor_scalar(mix[:, SSD_W + 256:], W[0][:, 0:256], sm["rs4"][:], None, ALU.mult), "mixed")
            yield "mix_t"
            for half in range(2):
                use = f"mix_t{half}"
                wait_full(dve, use)
                made(tt(hT[:, 4 * half:4 * half + 4], bank(use)[:].rearrange("p (k t) -> p k t", k=4),
                        over(catw[:, 4 * half:4 * half + 4], P)), "mixT")
            for half in range(2):
                yield f"out{2 * half + 1}"
                wait_full(dve, f"out{half}")
                xh = X[:, bass.ds(b, 1), half * 512:(half + 1) * 512].rearrange("p o d -> p (o d)")
                made(tt(xh, bank(f"out{half}")[:], xh, ALU.add), "x_mid")
            yield "norm2"
            mean("5", D)
            rstd("5")
            made(V.scalar_tensor_tensor(h2_next[:], Xb, sm["rs5"][:], n2w[:], ALU.mult, ALU.mult), "normed2")

            def top16(src, work, values, indices):
                chain(V.max(values[:, 0:8], src))
                chain(V.max_index(indices[:, 0:8], values[:, 0:8], src))
                chain(V.match_replace(work, values[:, 0:8], src, -3.0e38))
                chain(V.max(values[:, 8:16], work))
                chain(V.max_index(indices[:, 8:16], values[:, 8:16], work))

            for c in range(4):
                yield f"q{c}s"
                dve.wait_ge(sig("scores"), c + 1)
                for i in range(4):
                    top16(W[0][:, i * P:(i + 1) * P], W[9][:, 0:P], sv[:, 4 * c + i], si[:, 4 * c + i])
                made(V.tensor_copy(sif[:, 4 * c:4 * c + 4], si[:, 4 * c:4 * c + 4]), "top_keys")
            for h in range(PEER_H):
                yield f"pick{h}"
                cand = W[2][:, 0:256]
                chain(tt(cand.rearrange("p (i j) -> p i j", i=TOPK), sv[:, 2 * h].unsqueeze(2).to_broadcast([P, TOPK, TOPK]),
                         sv[:, 2 * h + 1].unsqueeze(1).to_broadcast([P, TOPK, TOPK]), ALU.add))
                top16(cand, W[3][:, 0:256], cv[:, h], ci[:, TOPK * h:TOPK * (h + 1)])
            yield "decode0"
            chain(V.tensor_scalar(ch[:, 0], ci[:], 4, None, ALU.logical_shift_right))
            chain(V.tensor_scalar(ch[:, 1], ci[:], TOPK - 1, None, ALU.bitwise_and))
            chain(V.tensor_copy(chf[:], ch[:]))
            for half in range(2):
                if half:
                    yield "decode1"
                chosen = sif[:].rearrange("p (h a) k -> p a h k", a=2)
                for quarter in range(4):
                    n = SLOTS // 4
                    eq = W[4][:].rearrange("p (s k) -> p s k", k=TOPK)
                    chain(tt(eq, chf[:, half, n * quarter:n * (quarter + 1)].unsqueeze(2).to_broadcast([P, n, TOPK]),
                             iota16.unsqueeze(1).to_broadcast([P, n, TOPK]), ALU.is_equal))
                    e4 = W[4][:].rearrange("p (h s k) -> p h s k", h=2, k=TOPK)
                    chain(tt(e4, e4, chosen[:, half, 2 * quarter:2 * quarter + 2].unsqueeze(2).to_broadcast([P, 2, TOPK, TOPK])))
                    chain(V.tensor_reduce(picked[:, half, n * quarter:n * (quarter + 1)], eq, AX.X, ALU.add))
            yield "gate"
            chain(V.scalar_tensor_tensor(picked[:, 1], picked[:, 0], float(KEYS), picked[:, 1], ALU.mult, ALU.add))
            chain(V.tensor_scalar(idx_next[:], picked[:, 1], const_at("first_row", step, 1), None, ALU.add))
            g3 = g_next[:].rearrange("p (h k) -> p h k", k=TOPK)
            made(tt(g3, cv[:], cv[:, :, 0:1].to_broadcast([P, PEER_H, TOPK]), ALU.subtract), "g_sub")
            dve.wait_ge(sig("g_exp"), 1)
            chain(V.tensor_reduce(sm["gsum"][:], g3, AX.X, ALU.add))
            chain(V.reciprocal(sm["grec"][:], sm["gsum"][:]))
            chain(tt(g3, g3, over(sm["grec"][:], TOPK)))

        class Phases:

            def __init__(self, part):
                self.part, self.at = part, next(part)

            def upto(self, last):
                while self.at is not None and ORDER[self.at] <= last:
                    before, self.at = self.at, next(self.part, None)
                    assert self.at is None or ORDER[self.at] > ORDER[before], (before, self.at)

        def phase_after(slot):
            return (slot + 1) * len(PHASES) // (SLOTS - 2)

        def step_program(mixing, gathering):
            with nc.Block() as block:
                @block.sync
                def _(sp):
                    if mixing:
                        mix_sync(sp, mixing[2])

                @block.gpsimd
                def _(pool):
                    if gathering is None:
                        return
                    pool.wait_ge(sig("idx_now"), 1)
                    for t in range(SLOTS + LAG):
                        if t < SLOTS:
                            if t >= U_RING:
                                pool.wait_ge(sig("u_used"), t - U_RING + 1)
                            pool.indirect_dma_start(
                                out=u_rows[:, t % U_RING, :], out_offset=None, in_=a["peer_u"],
                                in_offset=bass.IndirectOffsetOnAxis(ap=idx_now[:, t:t + 1], axis=0),
                            ).then_inc(u_in[t % U_RING], 16)
                        if t >= LAG:
                            s = t - LAG
                            if s >= V_RING:
                                pool.wait_ge(sig("v_used"), s - V_RING + 1)
                            pool.indirect_dma_start(
                                out=v_rows[:, s % V_RING, :], out_offset=None, in_=a["peer_v"],
                                in_offset=bass.IndirectOffsetOnAxis(ap=idx_now[:, s:s + 1], axis=0),
                            ).then_inc(v_in[s % V_RING], 16)

                @block.vector
                def _(dve):
                    chain = InOrder(dve, sig("vector_chain"))
                    phases = mixing and Phases(mix_vector(dve, mixing[1], mixing[0], chain))
                    if gathering is None:
                        phases.upto(len(PHASES))
                        return
                    made(V.tensor_copy(idx_now[:], idx_next[:]), "idx_now")
                    chain(V.tensor_copy(g_now[:], g_next[:]))
                    chain(V.tensor_copy(h2_now[:], h2_next[:]))
                    for s in range(SLOTS):
                        dve.wait_ge(u_in[s % U_RING], 16 * (s // U_RING + 1))
                        rows_u = u_rows[:, s % U_RING, :]
                        made(V.tensor_tensor_reduce(out=rows_u, in0=rows_u, in1=h2_now[:], scale=1.0, scalar=0.0,
                                                    op0=ALU.mult, op1=ALU.add, accum_out=dots[:, s:s + 1]), "u_used")
                        if s % TOPK == 1 and s > TOPK:
                            head = s // TOPK - 1
                            dve.wait_ge(sig("gelu"), head + 1)
                            cols = slice(head * TOPK, (head + 1) * TOPK)
                            made(V.tensor_tensor(wgt[:, cols], gel[:, cols], g_now[:, cols], ALU.mult), "weights")
                        if mixing:
                            phases.upto(phase_after(s))
                    dve.wait_ge(sig("gelu"), PEER_H)
                    made(V.tensor_tensor(wgt[:, SLOTS - TOPK:], gel[:, SLOTS - TOPK:], g_now[:, SLOTS - TOPK:], ALU.mult), "weights")
                    dve.wait_ge(sig("v_used"), SLOTS)
                    chain(V.tensor_copy(X[:, bass.ds(gathering, 1), :].rearrange("p o d -> p (o d)"), acc[:]))

                @block.scalar
                def _(act):
                    chain = InOrder(act, sig("scalar_chain"))
                    phases = mixing and Phases(mix_scalar(act, mixing[1], chain))
                    if gathering is None:
                        phases.upto(len(PHASES))
                        return
                    for s in range(SLOTS + LAG):
                        if s % TOPK == 0 and s > 0 and s <= SLOTS:
                            head = s // TOPK - 1
                            act.wait_ge(sig("u_used"), TOPK * (head + 1))
                            cols = slice(head * TOPK, (head + 1) * TOPK)
                            made(S.activation(gel[:, cols], dots[:, cols], ACT.Gelu), "gelu")
                        if s >= LAG:
                            t = s - LAG
                            act.wait_ge(sig("weights"), t // TOPK + 1)
                            if t >= DIAG_RING:
                                act.wait_ge(sig("v_used"), t - DIAG_RING + 1)
                            made(S.activation(diag[:, t % DIAG_RING], ident, ACT.Copy, scale=wgt[:, t:t + 1]), "diag")
                        if mixing and s < SLOTS:
                            phases.upto(phase_after(s))

                @block.tensor
                def _(pe):
                    phases = mixing and Phases(mix_tensor(pe, mixing[1]))
                    if gathering is None:
                        phases.upto(len(PHASES))
                        return
                    for half in range(2):
                        T.matmul(acc[:, half * 512:(half + 1) * 512], ident,
                                 X[:, bass.ds(gathering, 1), half * 512:(half + 1) * 512].rearrange("p o d -> p (o d)"),
                                 start=True, stop=False)
                    for s in range(SLOTS + LAG):
                        if s >= LAG:
                            t = s - LAG
                            pe.wait_ge(sig("diag"), t + 1)
                            pe.wait_ge(v_in[t % V_RING], 16 * (t // V_RING + 1))
                            for half in range(2):
                                last = T.matmul(acc[:, half * 512:(half + 1) * 512], diag[:, t % DIAG_RING],
                                                v_rows[:, t % V_RING, half * 512:(half + 1) * 512],
                                                start=False, stop=(t == SLOTS - 1))
                            made(last, "v_used")
                        if mixing and s < SLOTS:
                            phases.upto(phase_after(s))

        def clear():
            numbers = sorted(s.num for s in sems.values())
            assert numbers == list(range(numbers[0], numbers[0] + len(numbers)))
            nc.gpsimd.dma_reset(range(numbers[0], numbers[-1] + 1))
            nc.gpsimd.sem_clear(range(numbers[0], numbers[-1] + 1))
            nc.all_engine_barrier()

        with nc.Block() as block:
            @block.sync
            def _(sp):
                sp.dma_start(consts[:], const_dram).then_inc(sig("consts_in"), 16)
                sp.dma_start(X[:], x_dram.rearrange("o (b p) d -> (o p) b d", p=P)).then_inc(sig("x_in"), 16)
                sp.wait_ge(sig("consts_in"), 16)
                sp.wait_ge(sig("x_in"), 16)

            @block.gpsimd
            def _(pool):
                for tile in (state, xbcT, sbkT, sbv, nkT, nsv, kcvcT):
                    pool.memset(tile[:], 0.0)
        step_program((0, 0, 0), None)
        clear()
        with nc.Fori(0, STEPS - 1) as n:
            step_program((n + 1, (n + 1) % BLOCKS, (n + 1) // BLOCKS), n % BLOCKS)
            clear()
        step_program(None, BLOCKS - 1)
        with nc.Block() as block:
            @block.sync
            def _(sp):
                sp.dma_start(out_dram.rearrange("o (b p) d -> (o p) b d", p=P), X[:]).then_inc(sig("out_done"), 16)
                sp.wait_ge(sig("out_done"), 16)


_INS = ["x", "norm1_w", "w_in", "conv_w", "conv_b", "dt_bias", "a_log", "d_skip", "ssd_norm_w", "sb_out_w",
        "nsa_q_norm_w", "nsa_k_norm_w", "nsa_cmp_pos", "nsa_cmp_w", "nsa_out_w", "w_out", "norm2_w",
        "peer_w_q", "peer_sub_keys", "peer_u", "peer_v"]


def kernel(**inputs):
    import concourse.bacc as bacc
    from concourse.bass_utils import run_bass_kernel_spmd as run

    nc = bacc.Bacc("TRN2", target_bir_lowering=False, num_devices=1)
    arrays, aps = {}, {}
    for name in _INS:
        v = np.ascontiguousarray(inputs[name])
        if name in ("peer_u", "peer_v"):
            v = v.reshape(DEPTH * EXPERTS, D)
        arrays["in_" + name] = v
        aps[name] = nc.dram_tensor("in_" + name, v.shape, mybir.dt.float32, kind="ExternalInput").ap()
    arrays["constants"] = constants()
    const_dram = nc.dram_tensor("constants", arrays["constants"].shape, mybir.dt.float32, kind="ExternalInput").ap()
    out = nc.dram_tensor("out", (1, SEQ, D), mybir.dt.float32, kind="ExternalOutput").ap()
    trunk(nc, aps, const_dram, aps["x"], out)
    r = run(nc, [arrays], core_ids=[0])
    return r.results[0]["out"]
```

```python
from contextlib import ExitStack

import numpy as np
import concourse.bass as bass
from concourse import mybir

DEPTH, SEQ, D, P = 2, 512, 1024, 128
BLOCKS = SEQ // P
STEPS = DEPTH * BLOCKS
KT = D // P
HD = 64
SSD_W, SSD_H, SSD_N, TAPS = 512, 8, 128, 4
CONV_DIM = SSD_W + 4 * SSD_N
SB_H, NSA_H = 4, 4
IN_DIM = 2964
Z0, XS0, BC0, DT0, SBQ0, SBV0, KV0 = 0, 512, 1024, 1536, 1544, 2056, 2568
KVW = IN_DIM - KV0
CMP_LEN, CMP_STRIDE, CMP_PAD = 32, 16, 32
PEER_H, TOPK, KEYS, PEER_Q = 8, 16, 128, 2048
EXPERTS = KEYS * KEYS
SLOTS = PEER_H * TOPK
EPS = 1e-6
NEG = -1e30
SCALE = HD ** -0.5
U_RING, V_RING, DIAG_RING, W_RING = 5, 5, 3, 2
LAG = TOPK + 2
V_SHARE = 4
GATHER_TIME, DOT_TIME, SUM_TENSOR, SUM_VECTOR = 1.75, 1.2, 1.8, 1.3
V_PAUSE = range(88, 112)
BY_VECTOR = [s % V_SHARE == V_SHARE - 1 and s not in V_PAUSE for s in range(SLOTS)]

CONST = {}


def constants():
    i = np.arange(P)
    row, col = i[:, None], i[None, :]
    one, zero = np.ones((P, P)), np.zeros((P, P))
    pieces = {
        "ident": row == col,
        "tri": row <= col,
        "neg_tri_ge": -1.0 * (row >= col),
        "ones": one,
        "neg_ones": -one,
        "later": np.where(row > col, NEG, 0.0),
    }
    seen, unseen = [one] * (BLOCKS - 1), [zero] * (BLOCKS - 1)
    pieces["stay"] = np.concatenate([*seen, row < col, *unseen], 1)
    pieces["stay_neg"] = np.concatenate([*unseen, np.where(row < col, 0, NEG), *[NEG * one] * (BLOCKS - 1)], 1)
    pieces["causal_neg"] = np.concatenate([*unseen, np.where(col <= row, 0, NEG), *[NEG * one] * (BLOCKS - 1)], 1)
    last = np.arange(CMP_PAD) * CMP_STRIDE + CMP_LEN - 1
    token = np.arange(SEQ).reshape(BLOCKS, P).T[:, :, None, None]
    visible = np.broadcast_to(last[None, None, None, :] <= token, (P, BLOCKS, NSA_H, CMP_PAD)).reshape(P, -1)
    pieces["cmp_neg"] = np.where(visible, 0.0, NEG)
    pieces["cmp_seen"] = visible
    pieces["head_of"] = (row // CMP_PAD) == np.arange(NSA_H)[None, :]
    inv = np.float32(500000.0) ** (-np.arange(0, 16, 2, dtype=np.float32) / np.float32(16))
    angle = (np.arange(SEQ, dtype=np.float32)[:, None] * inv[None, :]).astype(np.float32)
    rope = np.concatenate([np.cos(angle), np.sin(angle)], 1).reshape(BLOCKS, P, 16)
    pieces["rope"] = rope.transpose(1, 0, 2).reshape(P, -1)
    pieces["iota"] = np.broadcast_to(np.arange(TOPK), (P, TOPK))
    steps = np.arange(STEPS)
    pieces["carry"] = np.broadcast_to(steps % BLOCKS != 0, (P, STEPS))
    pieces["first_row"] = np.broadcast_to(steps // BLOCKS * EXPERTS, (P, STEPS))
    at, parts = 0, []
    for name, piece in pieces.items():
        piece = np.asarray(piece, np.float32)
        CONST[name] = (at, at + piece.shape[1])
        at += piece.shape[1]
        parts.append(piece)
    return np.ascontiguousarray(np.concatenate(parts, 1))


A_PHASES, T_PHASES, R_PHASES = 15, 15, 17
HOP = .5
R_VECTOR = [0] * 7 + [3, 3] + [6.2] * 6 + [3.5, 3.5]
PHASES = (
    [("n1a", 1.5, .6), ("n1b", .3, .1), ("n1c", .3, .1), ("n1d", .8, .7), ("n1t", 1.8, 0), ("n1e", .4, 1.2)]
    + [("xs0", 3.5, 0), ("xs1", 3.5, 0), ("bc0", 3.5, 0), ("params", .5, 0), ("bc1", 3.5, 0), ("sbqk0", 3.5, 0)]
    + [("conv0", 0, 2), ("sbqk1", 3.5, 0), ("conv1", 0, 2), ("z0", 3.5, 0), ("conv2", 0, 2), ("z1", 3.5, 0)]
    + [("conv3", 0, 2), ("vq0", 3.5, 0), ("conv_out", 0, .2), ("vq1", 3.5, 0), ("kv0", 4, .7), ("kv1", 3, 0)]
    + [("a0", 1, .7), ("a1", 1, 0), ("a2", 1.8, 2.4), ("a3", 7, 1.2), ("a4", 4, 1.4), ("a5", 6, 1.8), ("a6", 5, 1.9)]
    + [("a7", 1.2, 1.2), ("a8", 1.2, 1.2), ("a9", .8, 1.8), ("a10", 0, 1.3), ("a11", 0, .8), ("a12", 0, .5)]
    + [("a13", 0, .4), ("a14", 0, .5), ("nt", 1.5, 0), ("ne", 0, .5), ("cmp_z", 0, 1.2)]
    + [(f"cmp{i}", 3.4, 0) for i in range(4)]
    + [(f"t{k}", 3 if k < 8 else 1.2, .8) for k in range(T_PHASES)]
    + [("nsum0", 0, 1.5), ("nsum1", 0, 0), ("nsum2", 0, .1), ("nsum3", 0, 0), ("nsum4", 0, .3), ("mt", 1.8, 0), ("me", 0, 1.2)]
    + [("out0", 3.5, 0), ("out1", 3.5, 0), ("out2", 3.5, .6), ("out3", 3.5, 0), ("oe", 0, .6)]
    + [("n2a", 0, 0), ("n2b", 0, .1), ("n2c", 0, 0), ("n2d", 0, 1.3), ("n2t", 1.8, 0), ("n2e", .4, 0)]
    + [(f"r{k}", 3.4 + .9 * (3 <= k and k % 2) if k < 8 else .5, R_VECTOR[k]) for k in range(R_PHASES)]
    + [(f"dec{i}", 0, 2.8) for i in range(8)] + [("gate0", 0, .6), ("gate1", 0, 0), ("gate2", 0, .6)]
)
ORDER = {name: i for i, (name, *_) in enumerate(PHASES)}
assert len(ORDER) == len(PHASES)
WORK = np.cumsum([max(work) + HOP for _, *work in PHASES])


def spare():
    slot = np.arange(SLOTS + LAG)
    u, v = np.minimum(slot + 1, SLOTS), np.maximum(slot + 1 - LAG, 0)
    time = GATHER_TIME * (u + v)
    by_vector = np.array([sum(BY_VECTOR[:n]) for n in v])
    tensor, vector = SUM_TENSOR * (v - by_vector), DOT_TIME * u + SUM_VECTOR * by_vector
    return 2 * time - tensor - vector


SPARE = spare()
PACE = .97 * SPARE[-1] / WORK[-1]

BANKS = [
    [("params", "params_out", 1), ("sbqk", "sb_qk", 2), ("cumsum", "acs", 1), ("l1", "decay", 2), ("y_off", "y_part", 1),
     ("state", "state_new", 1), ("cmp_tt", "v_bd", 1), ("cmp_kt", "kbd", 1), ("cmp_s", "cmp_sub", 1), ("cmp_pt", "cmp_pT", 1),
     ("cmp_o", "o_cmp", 1), ("mix_t0", "mixT", 1), ("q0", "q_tm", 1), ("q2", "q_tm", 3)],
    [("keys", "keys_out", 1), ("z", "z_silu", 1), ("l0", "decay", 1), ("cb", "decayed", 2), ("y_diag", "y", 1),
     ("n_t", "nkT", 1), ("s0", "probs", 1), ("s3", "probs", 4), ("s6", "probs", 7), ("mix_t1", "mixT", 2),
     ("q1", "q_tm", 2), ("q3", "q_tm", 4)],
    [("h_t0", "hT", 1), ("vq", "vq_read", 1), ("sbz0", "sb_log", 1), ("sbz2", "sb_log", 3), ("kcvc_t", "kcvcT", 1),
     ("s1", "probs", 2), ("s4", "probs", 5), ("s7", "probs", 8), ("out0", "x_mid", 1), ("qt0", "qT", 1), ("qt2", "qT", 3)],
    [("h_t1", "hT", 2), ("xs_t", "xs_tm", 1), ("sbz1", "sb_log", 2), ("sbz3", "sb_log", 4), ("cmp_k", "cmp_rep", 1),
     ("s2", "probs", 3), ("s5", "probs", 6), ("out1", "x_mid", 2), ("qt1", "qT", 2), ("qt3", "qT", 4)],
    [("xs", "xbc_in", 1), ("b_t", "b_tm", 1)] + [(f"sbr{h}", "sb_w", h + 1) for h in range(SB_H)]
    + [("cmp_v", "cmp_rep", 2)] + [(f"p{i}", "probsT", i + 1) for i in range(2 * NSA_H)]
    + [("h2_t0", "h2T", 1), ("sc0", "scores", 1), ("sc2", "scores", 3)],
    [("bc", "xbc_in", 2), ("kv", "kv_read", 1), ("sb_o", "mixed_sb", 1), ("att_o", "att_read", 1), ("h2_t1", "h2T", 2),
     ("sc1", "scores", 2), ("sc3", "scores", 4)],
]
BANK_OF = {use[0]: n for n, uses in enumerate(BANKS) for use in uses}
USE_OF = {use[0]: i + 1 for uses in BANKS for i, use in enumerate(uses)}


def trunk(nc, a, const_dram, x_dram, out_dram):
    fp32, u32 = mybir.dt.float32, mybir.dt.uint32
    ALU, ACT, AX = mybir.AluOpType, mybir.ActivationFunctionType, mybir.AxisListType
    V, S, T = nc.vector, nc.scalar, nc.tensor
    ctx = ExitStack()
    with ctx:
        def sb(name, shape, dt=fp32):
            return ctx.enter_context(nc.sbuf_tensor(name, shape, dt))

        width = max(hi for _, hi in CONST.values())
        consts = sb("consts", [P, width])

        def const(name):
            lo, hi = CONST[name]
            return consts[:, lo:hi]

        def const_at(name, block, n):
            lo, _ = CONST[name]
            return consts[:, bass.ds(lo + block, n)]

        ident, tri, iota16 = const("ident"), const("tri"), const("iota")
        X = sb("X", [P, BLOCKS, D])
        w_ring = sb("w_ring", [P, W_RING, KT, 512])
        u_rows = sb("u_rows", [P, U_RING, D])
        v_rows = sb("v_rows", [P, V_RING, D])
        diag = sb("diag", [P, DIAG_RING, P])
        mix = sb("mix", [P, D])
        scratch = sb("scratch", [P, D])
        hT = sb("hT", [P, KT, P])
        h2_next, h2_now = sb("h2_next", [P, D]), sb("h2_now", [P, D])
        xbcT = sb("xbcT", [P, KT, P + TAPS - 1])
        xbc = sb("xbc", [P, KT, P])
        state = sb("state", [P, SSD_W])
        sbqT, sbkT, sbv = sb("sbqT", [P, 2, P]), sb("sbkT", [P, 2, SEQ]), sb("sbv", [P, BLOCKS, 256])
        nqk = sb("nqk", [P, 7, HD])
        kcvc = sb("kcvc", [P, 2, HD])
        kk = sb("kk", [P, 2, 2, HD])
        nqT, nkT, nsv = sb("nqT", [P, 2, P]), sb("nkT", [P, 2, SEQ]), sb("nsv", [P, BLOCKS, P])
        kcvcT = sb("kcvcT", [P, SEQ + CMP_STRIDE])
        rope = sb("rope", [P, 2, 8])
        r = sb("r", [P, 4, 7, 8])
        W = [sb(f"w{i}", [P, 512]) for i in range(10)]
        b_tm = sb("b_tm", [P, 2, SSD_N])
        sb_ln = [hT[:, 4 * i:4 * i + 4].rearrange("p k t -> p (k t)") for i in range(2)]
        sb_relu = [h2_next[:, 512 * i:512 * i + 512] for i in range(2)]
        sb_sp = [W[8][:], W[9][:]]
        sb_wT = [scratch[:, 0:512], xbc[:, 0:4].rearrange("p i t -> p (i t)")]
        junk = scratch[:, 512:1024]
        cmp_z = hT[:].rearrange("p k t -> p (k t)").rearrange("p (j c) -> p j c", j=CMP_LEN)
        rows = sb("rows", [40, P])
        pos_rows = sb("pos_rows", [CMP_LEN, 2, HD])
        key_rows = sb("key_rows", [P, 2, P])
        conv_p, posT, keysT = sb("conv_p", [P, 40]), sb("posT", [P, CMP_LEN]), sb("keysT", [P, 2, P])
        n1w, catw = sb("n1w", [P, KT]), sb("catw", [P, KT])
        n2w = sb("n2w", [P, D])
        dtb, alog, dskip = sb("dtb", [P, SSD_H]), sb("alog", [P, SSD_H]), sb("dskip", [P, SSD_H])
        qkw = sb("qkw", [P, 7, HD])
        sm = {n: sb("sm_" + n, [P, c]) for n, c in dict(
            ss1=1, ms1=1, rt1=1, rs1=1, ss2=1, ms2=1, rt2=1, rs2=1, ss3=1, ms3=1, rt3=1, rs3=1, ss4=1, ms4=1, rt4=1,
            rs4=1, ss5=1, ms5=1, rt5=1, rs5=1, ssq=6, msq=6, rtq=6, rsq=6, ssc=1, msc=1, rtc=1, rsc=1,
            dtp=8, dta=8, dt=8, ea=8, dtA=8, acs=24, nacs=8, ed=24, gt=12, sg=12, mx=8, nm=8, sums=8, coef=8,
            cm=4, csum=4, crec=4, gsum=8, grec=8).items()}
        kn = sb("kn", [P, HD])
        k2 = sb("k2", [64, 2, HD])
        kbd = sb("kbd", [P, 64])
        sv = sb("sv", [P, 2 * PEER_H, TOPK])
        si = sb("si", [P, 2 * PEER_H, TOPK], u32)
        sif = sb("sif", [P, 2 * PEER_H, TOPK])
        cv = sb("cv", [P, PEER_H, TOPK])
        ci = sb("ci", [P, SLOTS], u32)
        ch = sb("ch", [P, 2, SLOTS], u32)
        chf = sb("chf", [P, 2, SLOTS])
        picked = sb("picked", [P, 2, SLOTS])
        idx_next, idx_now = sb("idx_next", [P, SLOTS], u32), sb("idx_now", [P, SLOTS], u32)
        g_next, g_now = sb("g_next", [P, SLOTS]), sb("g_now", [P, SLOTS])
        dots, gel, wgt = sb("dots", [P, SLOTS]), sb("gel", [P, SLOTS]), sb("wgt", [P, SLOTS])

        acc_v = sb("acc_v", [P, D])

        acc = ctx.enter_context(nc.psum_tensor("acc", [P, D], fp32))
        banks = [ctx.enter_context(nc.psum_tensor(f"bank{i}", [P, 512], fp32)) for i in range(6)]

        def bank(use):
            return banks[BANK_OF[use]]

        sems = {}

        def sig(name):
            if name not in sems:
                sems[name] = ctx.enter_context(nc.semaphore(name))
            return sems[name]

        u_in = [sig(f"u_in{i}") for i in range(U_RING)]
        v_in = [sig(f"v_in{i}") for i in range(V_RING)]
        for i in range(6):
            sig(f"bank{i}_full")
        w_in = [sig(f"w_in{i}") for i in range(W_RING)]

        def made(ins, name):
            return ins.then_inc(sig(name), 1)

        def full(ins, use):
            return ins.then_inc(sig(f"bank{BANK_OF[use]}_full"), 1)

        def wait_full(eng, use):
            eng.wait_ge(sig(f"bank{BANK_OF[use]}_full"), USE_OF[use])

        def wait_free(pe, use):
            if USE_OF[use] > 1:
                _, by, count = BANKS[BANK_OF[use]][USE_OF[use] - 2]
                pe.wait_ge(sig(by), count)

        class InOrder:

            def __init__(self, eng, sem):
                self.eng, self.sem, self.n = eng, sem, 0

            def __call__(self, ins):
                self.n += 1
                ins.then_inc(self.sem, 1)
                self.eng.wait_ge(self.sem, self.n)

        CHUNKS = [("in", XS0), ("in", BC0), ("in", SBQ0), ("in", Z0), ("in", SBV0), ("kv", 0), ("cmp", 0),
                  ("out", 0), ("out", 512), ("q", 0), ("q", 512), ("q", 1024), ("q", 1536)]

        CHUNK_USES = ["xs", "bc", "sbqk", "z", "vq", "kv", "cmp_v", "out0", "out1", "q0", "q1", "q2", "q3"]

        def chunk(c):
            return w_ring[:, c % W_RING]

        def wait_chunk(pe, c):
            count = sum(16 * (2 if CHUNKS[k][0] in ("kv", "cmp") else 1) for k in range(c % W_RING, c + 1, W_RING))
            pe.wait_ge(w_in[c % W_RING], count)

        def mix_sync(sp, l):
            def param(dst, src):
                sp.dma_start(dst, src).then_inc(sig("params_in"), 16)

            lw = bass.ds(l, 1)

            def one(src, pattern, **k):
                return src[lw].rearrange("o " + pattern, **k)

            sp.dma_start(n1w[:], one(a["norm1_w"], "(p k) -> (o p) k", k=KT)).then_inc(sig("n1w_in"), 16)
            for c, (what, c0) in enumerate(CHUNKS):
                if c == W_RING:
                    param(rows[0:32, :], one(a["conv_w"], "t (i c) -> (o t i) c", c=P))
                    param(rows[32:40, :], one(a["conv_b"], "(i c) -> (o i) c", c=P))
                    param(pos_rows[:], one(a["nsa_cmp_pos"], "i j d -> (o j) i d"))
                    param(key_rows[:], one(a["peer_sub_keys"], "h k d -> (o k) h d"))
                    param(catw[0:64, :], one(a["ssd_norm_w"], "(p k) -> (o p) k", k=KT))
                    param(catw[64:96, :], one(a["sb_out_w"], "(p k) -> (o p) k", k=KT))
                    param(catw[96:128, :], one(a["nsa_out_w"], "(p k) -> (o p) k", k=KT))
                    for dst, src in ((n2w, "norm2_w"), (dtb, "dt_bias"), (alog, "a_log"), (dskip, "d_skip")):
                        param(dst[:], a[src][lw].to_broadcast([P, dst.shape[1]]))
                    param(qkw[:, 0:3, :], one(a["nsa_k_norm_w"], "r d -> o (r d)").to_broadcast([P, 3 * HD]))
                    for h in range(NSA_H):
                        param(qkw[:, 3 + h, :], a["nsa_q_norm_w"][lw].to_broadcast([P, HD]))
                if c >= W_RING:
                    wait_full(sp, CHUNK_USES[c - W_RING])
                dst = chunk(c)
                done = w_in[c % W_RING]
                if what == "in":
                    sp.dma_start(dst, one(a["w_in"], "(p k) n -> (o p) k n", k=KT)[:, :, c0:c0 + 512]).then_inc(done, 16)
                elif what == "kv":
                    wi = one(a["w_in"], "(p k) n -> (o p) k n", k=KT)
                    sp.dma_start(dst[:, :, 0:8], wi[:, :, DT0:DT0 + 8]).then_inc(done, 16)
                    sp.dma_start(dst[:, :, 8:8 + KVW], wi[:, :, KV0:IN_DIM]).then_inc(done, 16)
                elif what == "cmp":
                    flat = dst.rearrange("p k n -> p (k n)")[:, 0:CMP_LEN * HD].rearrange("p (j e) -> p j e", e=HD)
                    for i in range(2):
                        sp.dma_start(flat[64 * i:64 * i + 64],
                                     a["nsa_cmp_w"][lw, i].rearrange("o (j d) e -> (o d) j e", d=HD)).then_inc(done, 16)
                elif what == "out":
                    sp.dma_start(dst, one(a["w_out"], "(p k) n -> (o p) k n", k=KT)[:, :, c0:c0 + 512]).then_inc(done, 16)
                else:
                    sp.dma_start(dst, one(a["peer_w_q"], "(p k) n -> (o p) k n", k=KT)[:, :, c0:c0 + 512]).then_inc(done, 16)

        PARAMS = 11 + 1 + NSA_H

        def mix_tensor(pe, b, seen):
            keys = slice(0, seen * P)

            def transposes(use, tiles, n=P):
                for i, tile in enumerate(tiles):
                    last = T.transpose(bank(use)[:, i * n:(i + 1) * n], tile, ident)
                return full(last, use)

            def h_transposed(src, names, ready):
                pe.wait_ge(sig(ready), 1)
                v = src[:].rearrange("p (f k) -> p k f", k=KT)
                for half, use in enumerate(names):
                    wait_free(pe, use)
                    transposes(use, [v[:, 4 * half + i] for i in range(4)])

            def features(use, c, lo, hi):
                if lo == 0:
                    wait_free(pe, use)
                    wait_chunk(pe, c)
                for m in range(lo, hi):
                    for k in range(KT):
                        last = T.matmul(bank(use)[:, m * P:(m + 1) * P], chunk(c)[:, k, m * P:(m + 1) * P], hT[:, k, :],
                                        start=(k == 0), stop=(k == KT - 1))
                if hi == 4:
                    full(last, use)

            def tokens(use, c, lo, hi, n=512):
                if lo == 0:
                    wait_free(pe, use)
                    wait_chunk(pe, c)
                for k in range(lo, hi):
                    last = T.matmul(bank(use)[:, 0:n], hT[:, k, :], chunk(c)[:, k, 0:n], start=(k == 0), stop=(k == KT - 1))
                if hi == KT:
                    full(last, use)

            def params():
                pe.wait_ge(sig("params_in"), 16 * PARAMS)
                T.transpose(bank("params")[:, 0:40], rows[:], ident[0:40, 0:40])
                full(T.transpose(bank("params")[:, 64:96], pos_rows[:].rearrange("j i d -> j (i d)"), ident[0:32, 0:32]), "params")
                transposes("keys", [key_rows[:, i] for i in range(2)])

            yield "n1t"
            h_transposed(mix, ("h_t0", "h_t1"), "normed1")
            for c, (use, ready) in enumerate((("xs", "hT"), ("bc", None), ("sbqk", None))):
                yield f"{use}0"
                if ready:
                    pe.wait_ge(sig(ready), 2)
                features(use, c, 0, 2)
                if use == "bc":
                    yield "params"
                    params()
                yield f"{use}1"
                features(use, c, 2, 4)
            for c, use in ((3, "z"), (4, "vq"), (5, "kv")):
                n = 512 if use != "kv" else 8 + KVW
                yield f"{use}0"
                tokens(use, c, 0, 4, n)
                if use == "kv":
                    pe.wait_ge(sig("xbc"), 1)
                    wait_free(pe, "xs_t")
                    transposes("xs_t", [xbc[:, i] for i in range(4)])
                    wait_free(pe, "b_t")
                    transposes("b_t", [xbc[:, 4 + g] for g in range(2)])
                yield f"{use}1"
                tokens(use, c, 4, 8, n)

            def decay_scores(g):
                use = f"l{g}"
                wait_free(pe, use)
                out = bank(use)[:].rearrange("p (h l) -> p h l", h=4)
                T.matmul(out, ident, const("later").unsqueeze(1).to_broadcast([P, 4, P]), start=True, stop=False)
                for h in range(4):
                    last = T.matmul(out[:, h], sm["dtA"][:, 4 * g + h:4 * g + h + 1].to_broadcast([P, P]), tri,
                                    start=False, stop=(h == 3))
                full(last, use)

            def ssd(k):
                if k == 3:
                    pe.wait_ge(sig("dtA"), 1)
                    wait_free(pe, "cumsum")
                    T.matmul(bank("cumsum")[:, 0:8], tri, sm["dtA"][:], start=True, stop=True)
                    full(T.matmul(bank("cumsum")[:, 8:16], const("ones"), sm["dtA"][:], start=True, stop=True), "cumsum")
                    decay_scores(0)
                elif k == 5:
                    decay_scores(1)
                elif k == 6:
                    wait_free(pe, "cb")
                    for g in range(2):
                        last = T.matmul(bank("cb")[:, g * P:(g + 1) * P], xbc[:, 4 + g], xbc[:, 6 + g], start=True, stop=True)
                    full(last, "cb")
                elif k == 7:
                    wait_free(pe, "y_off")
                    pe.wait_ge(sig("state_kept"), 1)
                    for g in range(2):
                        last = T.matmul(bank("y_off")[:, 256 * g:256 * g + 256], xbc[:, 6 + g], state[:, 256 * g:256 * g + 256],
                                        start=True, stop=True)
                    full(last, "y_off")
                elif k == 8:
                    wait_free(pe, "y_diag")
                    pe.wait_ge(sig("decayed"), 2)
                    for h in range(SSD_H):
                        at = slice(h * HD, (h + 1) * HD)
                        last = T.matmul(bank("y_diag")[:, at], W[4 + h // 4][:, h % 4 * P:(h % 4 + 1) * P], W[2][:, at],
                                        start=True, stop=True)
                    full(last, "y_diag")
                elif k == 9:
                    wait_free(pe, "state")
                    pe.wait_ge(sig("b_tm"), 1)
                    pe.wait_ge(sig("x_dec"), 1)
                    for g in range(2):
                        last = T.matmul(bank("state")[:, 256 * g:256 * g + 256], b_tm[:, g], W[3][:, 256 * g:256 * g + 256],
                                        start=True, stop=True)
                    full(last, "state")

            def sb_scores(use, h, start):
                base, hp = 64 * (h % 2), h // 2
                for kb in range(seen):
                    last = T.matmul(bank(use)[:, kb * P:(kb + 1) * P], sbkT[base:base + 64, hp, kb * P:(kb + 1) * P],
                                    sbqT[base:base + 64, hp, :], start=start, stop=start)
                return last

            def sb(k):
                if k < SB_H:
                    if k == 0:
                        pe.wait_ge(sig("sb_qk"), 2)
                    wait_free(pe, f"sbz{k}")
                    full(sb_scores(f"sbz{k}", k, True), f"sbz{k}")
                if 0 <= k - 5 < SB_H:
                    h = k - 5
                    if h == 0:
                        wait_free(pe, "sb_o")
                        pe.wait_ge(sig("sb_v"), 1)
                    pe.wait_ge(sig("sb_w"), h + 1)
                    for kb in range(seen):
                        last = T.matmul(bank("sb_o")[:, h * HD:(h + 1) * HD], sb_wT[h % 2][:, kb * P:(kb + 1) * P],
                                        sbv[:, kb, h * HD:(h + 1) * HD], start=(kb == 0), stop=(kb == seen - 1))
                    if h == SB_H - 1:
                        full(last, "sb_o")
                    else:
                        made(last, "sb_head")
                if 0 <= k - 3 < SB_H:
                    h = k - 3
                    use = f"sbr{h}"
                    wait_free(pe, use)
                    T.matmul(bank(use)[:, keys], ident, const_at("stay_neg", (BLOCKS - 1 - b) * P, seen * P), start=True, stop=False)
                    sb_scores(use, h, False)
                    pe.wait_ge(sig("softplus"), h + 1)
                    last = T.matmul(bank(use)[:, keys], const("neg_tri_ge"), sb_sp[h % 2][:, keys], start=False, stop=(seen == 1))
                    for kb in range(1, seen):
                        last = T.matmul(bank(use)[:, 0:kb * P].rearrange("p (k q) -> p k q", k=kb), const("neg_ones"),
                                        sb_sp[h % 2][:, kb * P:(kb + 1) * P].unsqueeze(1).to_broadcast([P, kb, P]),
                                        start=False, stop=(kb == seen - 1))
                    full(last, use)

            for k in range(A_PHASES):
                yield f"a{k}"
                ssd(k)
                sb(k)

            yield "nt"
            pe.wait_ge(sig("roped"), 1)
            wait_free(pe, "n_t")
            q2 = nqk[:, 3:7, :].rearrange("p h d -> p (h d)")
            transposes("n_t", [q2[:, 0:P], q2[:, P:2 * P], kk[:, 0].rearrange("p a d -> p (a d)"),
                               kk[:, 1].rearrange("p a d -> p (a d)")])
            wait_free(pe, "kcvc_t")
            transposes("kcvc_t", [kcvc[:].rearrange("p a d -> p (a d)")])
            cmp_w = chunk(6).rearrange("p k n -> p (k n)")[:, 0:CMP_LEN * HD].rearrange("p (j e) -> p j e", e=HD)
            for i in range(4):
                yield f"cmp{i}"
                if i == 0:
                    pe.wait_ge(sig("cmp_z"), 1)
                    wait_chunk(pe, 6)
                    wait_free(pe, "cmp_k")
                    wait_free(pe, "cmp_v")
                for j in range(8 * i, 8 * i + 8):
                    for use, lo in (("cmp_k", 0), ("cmp_v", 64)):
                        last = T.matmul(bank(use)[0:64, 0:CMP_PAD], cmp_w[lo:lo + 64, j, :], cmp_z[lo:lo + 64, j, :],
                                        start=(j == 0), stop=(j == CMP_LEN - 1))
                        if j == CMP_LEN - 1:
                            full(last, use)

            def compressed(k):
                if k == 1:
                    wait_free(pe, "cmp_tt")
                    pe.wait_ge(sig("cmp_rep"), 2)
                    for kv in range(2):
                        last = T.transpose(bank("cmp_tt")[:, kv * HD:(kv + 1) * HD], W[6][0:64, kv * P:(kv + 1) * P],
                                           ident[0:64, 0:64])
                    full(last, "cmp_tt")
                elif k == 5:
                    wait_free(pe, "cmp_kt")
                    pe.wait_ge(sig("k2"), 1)
                    full(T.transpose(bank("cmp_kt")[:, 0:64], k2[:].rearrange("p a d -> p (a d)"), ident[0:64, 0:64]), "cmp_kt")
                elif k == 7:
                    wait_free(pe, "cmp_s")
                    pe.wait_ge(sig("kbd"), 1)
                    T.matmul(bank("cmp_s")[:, 0:P], ident, const_at("cmp_neg", b * P, P), start=True, stop=False)
                    for hp in range(2):
                        last = T.matmul(bank("cmp_s")[:, 64 * hp:64 * hp + 64], nqT[:, hp], kbd[:], start=False, stop=(hp == 1))
                    full(last, "cmp_s")
                elif k == 11:
                    wait_free(pe, "cmp_pt")
                    pe.wait_ge(sig("cmp_p"), 1)
                    transposes("cmp_pt", [W[7][:, 0:P]])
                elif k == 13:
                    wait_free(pe, "cmp_o")
                    pe.wait_ge(sig("cmp_pT"), 1)
                    full(T.matmul(bank("cmp_o")[:, 0:256], W[8][:, 0:P], W[9][:, 0:256], start=True, stop=True), "cmp_o")

            units = 2 * NSA_H

            def attention(k):
                if k < units:
                    br, h = k // NSA_H, k % NSA_H
                    base, use = 64 * (h % 2), f"s{k}"
                    if k == 0:
                        pe.wait_ge(sig("nqT"), 1)
                        pe.wait_ge(sig("nkT"), 1)
                    wait_free(pe, use)
                    T.matmul(bank(use)[:, keys], ident, const_at("causal_neg", (BLOCKS - 1 - b) * P, seen * P), start=True, stop=False)
                    full(T.matmul(bank(use)[:, keys], nqT[base:base + 64, h // 2], nkT[base:base + 64, br, keys],
                                  start=False, stop=True), use)
                if 0 <= k - 5 < units:
                    j = k - 5
                    br = j // NSA_H
                    if j == 0:
                        wait_free(pe, "att_o")
                    pe.wait_ge(sig("probsT"), j + 1)
                    for kb in range(seen):
                        last = T.matmul(bank("att_o")[:, j * HD:(j + 1) * HD], W[4 + j % 2][:, kb * P:(kb + 1) * P],
                                        nsv[:, kb, br * HD:(br + 1) * HD], start=(kb == 0), stop=(kb == seen - 1))
                    if j == units - 1:
                        full(last, "att_o")
                    else:
                        made(last, "att_head")
                if 0 <= k - 3 < units:
                    use = f"p{k - 3}"
                    wait_free(pe, use)
                    pe.wait_ge(sig("probs"), k - 2)
                    transposes(use, [W[2 + (k - 3) % 2][:, kb * P:(kb + 1) * P] for kb in range(seen)])

            for k in range(T_PHASES):
                yield f"t{k}"
                compressed(k)
                attention(k)
            yield "mt"
            pe.wait_ge(sig("mixed_ssd"), 1)
            pe.wait_ge(sig("mixed_sb"), 1)
            h_transposed(mix, ("mix_t0", "mix_t1"), "mixed_nsa")
            for i in range(4):
                yield f"out{i}"
                if i == 0:
                    pe.wait_ge(sig("mixT"), 2)
                tokens(f"out{i // 2}", 7 + i // 2, 4 * (i % 2), 4 * (i % 2) + 4)
            yield "n2t"
            h_transposed(h2_next, ("h2_t0", "h2_t1"), "normed2")

            for k in range(R_PHASES):
                yield f"r{k}"
                turn, score = (k - 3) // 2, (k - 5) // 2
                if k % 2 and 0 <= turn < 4:
                    wait_free(pe, f"qt{turn}")
                    pe.wait_ge(sig("q_tm"), turn + 1)
                    transposes(f"qt{turn}", [W[6][:, i * P:(i + 1) * P] for i in range(4)])
                if k % 2 and 0 <= score < 4:
                    wait_free(pe, f"sc{score}")
                    pe.wait_ge(sig("qT"), score + 1)
                    pe.wait_ge(sig("keys_out"), 1)
                    for i in range(4):
                        last = T.matmul(bank(f"sc{score}")[:, i * P:(i + 1) * P], W[8][:, i * P:(i + 1) * P], keysT[:, i % 2],
                                        start=True, stop=True)
                    full(last, f"sc{score}")
                if k < 8:
                    if k == 0:
                        pe.wait_ge(sig("h2T"), 2)
                    tokens(f"q{k // 2}", 9 + k // 2, 4 * (k % 2), 4 * (k % 2) + 4)

        def mix_scalar(act, b, seen, chain):
            keys = slice(0, seen * P)

            def copy(dst, src, **k):
                return S.activation(dst, src, ACT.Copy, **k)

            def root(n):
                act.wait_ge(sig("mean" + n), 1)
                made(S.activation(sm["rt" + n][:], sm["ms" + n][:], ACT.Sqrt), "root" + n)

            def squares(n, src, width, out):
                S.activation(out, src, ACT.Square, accum_out=sm["ss" + n][:]).then_inc(sig("squares" + n), 1)

            Xb = X[:, bass.ds(b, 1), :].rearrange("p o d -> p (o d)")
            yield "n1a"
            squares("1", Xb, D, scratch[:])
            yield "n1c"
            root("1")
            yield "bc0"
            wait_full(act, "xs")
            made(copy(xbcT[:, 0:4, TAPS - 1:], bank("xs")[:].rearrange("p (i t) -> p i t", i=4)), "xbc_in")
            yield "bc1"
            wait_full(act, "params")
            chain(copy(conv_p[:], bank("params")[:, 0:40]))
            made(copy(posT[:], bank("params")[:, 64:96]), "params_out")
            wait_full(act, "keys")
            made(copy(keysT[:].rearrange("p a d -> p (a d)"), bank("keys")[:, 0:256]), "keys_out")
            yield "sbqk0"
            wait_full(act, "bc")
            made(copy(xbcT[:, 4:8, TAPS - 1:], bank("bc")[:].rearrange("p (i t) -> p i t", i=4)), "xbc_in")
            yield "z0"
            wait_full(act, "sbqk")
            made(copy(sbqT[:].rearrange("p a q -> p (a q)"), bank("sbqk")[:, 0:256], scale=SCALE), "sb_qk")
            made(copy(sbkT[:, :, bass.ds(b * P, P)], bank("sbqk")[:, 256:512].rearrange("p (a q) -> p a q", a=2)), "sb_qk")
            yield "vq0"
            wait_full(act, "z")
            made(S.activation(W[0][:], bank("z")[:], ACT.Silu), "z_silu")
            yield "conv_out"
            act.wait_ge(sig("conv"), 8 * TAPS)
            made(S.activation(xbc[:].rearrange("p i t -> p (i t)"), scratch[:], ACT.Silu), "xbc")
            yield "kv1"
            wait_full(act, "xs_t")
            made(copy(W[1][:], bank("xs_t")[:]), "xs_tm")
            wait_full(act, "b_t")
            made(copy(b_tm[:].rearrange("p g n -> p (g n)"), bank("b_t")[:, 0:256]), "b_tm")

            def decays(g):
                wait_full(act, f"l{g}")
                for h in range(4):
                    last = S.activation(W[4 + g][:, h * P:(h + 1) * P], bank(f"l{g}")[:, h * P:(h + 1) * P], ACT.Exp,
                                        bias=sm["nacs"][:, 4 * g + h:4 * g + h + 1])
                    if h < 3:
                        made(last, "decay_head")
                made(last, "decay")

            def ssd(k):
                if k == 1:
                    act.wait_ge(sig("kv_read"), 1)
                    chain(S.activation(sm["dta"][:], sm["dtp"][:], ACT.Abs))
                    chain(S.activation(sm["dta"][:], sm["dta"][:], ACT.Exp, scale=-1.0))
                    chain(S.activation(sm["dta"][:], sm["dta"][:], ACT.Ln, bias=1.0))
                    chain(S.activation(sm["sg"][:], sm["gt"][:], ACT.Exp, scale=-1.0))
                    made(S.activation(sm["ea"][:], alog[:], ACT.Exp), "dt_log")
                elif k == 5:
                    act.wait_ge(sig("acs"), 1)
                    made(S.activation(sm["ed"][:], sm["acs"][:], ACT.Exp), "ed")
                    decays(0)
                elif k == 6:
                    decays(1)
                elif k == 11:
                    act.wait_ge(sig("y"), 1)
                    squares("2", W[6][:], SSD_W, junk)
                elif k == 13:
                    root("2")

            def sb(k):
                if 0 <= k - 4 < SB_H:
                    h = k - 4
                    wait_full(act, f"sbr{h}")
                    if h >= 2:
                        act.wait_ge(sig("sb_head"), h - 1)
                    made(S.activation(sb_wT[h % 2][:, keys], bank(f"sbr{h}")[:, keys], ACT.Exp), "sb_w")
                if 0 <= k - 1 < SB_H:
                    h = k - 1
                    z, ln = bank(f"sbz{h}")[:, keys], sb_ln[h % 2][:, keys]
                    wait_full(act, f"sbz{h}")
                    if h >= 2:
                        act.wait_ge(sig("softplus"), h - 1)
                    chain(S.activation(ln, z, ACT.Abs))
                    chain(S.activation(ln, ln, ACT.Exp, scale=-1.0))
                    chain(S.activation(ln, ln, ACT.Ln, bias=1.0))
                    made(S.activation(sb_relu[h % 2][:, keys], z, ACT.Relu), "sb_log")
                if k == 9:
                    wait_full(act, "sb_o")
                    squares("3", bank("sb_o")[:, 0:256], 256, sb_relu[0][:, 0:256])
                if k == 11:
                    root("3")

            for k in range(A_PHASES):
                yield f"a{k}"
                ssd(k)
                sb(k)
                if k == 4:
                    root("q")
            yield "ne"
            wait_full(act, "n_t")
            made(copy(nqT[:].rearrange("p a q -> p (a q)"), bank("n_t")[:, 0:256], scale=SCALE), "nqT")

            def compressed(k):
                if k == 3:
                    root("c")
                elif k == 6:
                    wait_full(act, "cmp_kt")
                    made(copy(kbd[:], bank("cmp_kt")[:, 0:64]), "kbd")
                elif k == 9:
                    act.wait_ge(sig("cmp_sub"), 1)
                    made(S.activation(W[7][:, 0:P], W[7][:, 0:P], ACT.Exp), "cmp_e")
                elif k == 12:
                    wait_full(act, "cmp_pt")
                    made(copy(W[8][:, 0:P], bank("cmp_pt")[:, 0:P]), "cmp_pT")

            units = 2 * NSA_H
            for k in range(T_PHASES):
                yield f"t{k}"
                if 0 <= k - 4 < units:
                    i = k - 4
                    wait_full(act, f"p{i}")
                    if i >= 2:
                        act.wait_ge(sig("att_head"), i - 1)
                    made(copy(W[4 + i % 2][:, keys], bank(f"p{i}")[:, keys]), "probsT")
                if 0 <= k - 2 < units:
                    i = k - 2
                    act.wait_ge(sig("row_max"), i + 1)
                    if i >= 2:
                        wait_full(act, f"p{i - 2}")
                    made(S.activation(W[2 + i % 2][:, keys], bank(f"s{i}")[:, keys], ACT.Exp, bias=sm["nm"][:, i:i + 1],
                                      accum_out=sm["sums"][:, i:i + 1]), "probs")
                compressed(k)
            yield "nsum1"
            act.wait_ge(sig("nsa_o"), 1)
            squares("4", W[0][:, 0:256], 256, junk[:, 0:256])
            yield "nsum3"
            root("4")
            yield "n2a"
            act.wait_ge(sig("x_mid"), 2)
            squares("5", Xb, D, scratch[:])
            yield "n2c"
            root("5")
            yield "n2e"
            for half in range(2):
                wait_full(act, f"h2_t{half}")
                made(copy(hT[:, 4 * half:4 * half + 4].rearrange("p k t -> p (k t)"), bank(f"h2_t{half}")[:]), "h2T")
            for k in range(R_PHASES):
                yield f"r{k}"
                if k % 2 == 0 and 0 <= (k - 6) // 2 < 4:
                    c = (k - 6) // 2
                    wait_full(act, f"sc{c}")
                    if c >= 2:
                        act.wait_ge(sig("top_keys"), c - 1)
                    made(copy(W[c % 2][:], bank(f"sc{c}")[:]), "scores")
                if k % 2 == 0 and 0 <= (k - 4) // 2 < 4:
                    c = (k - 4) // 2
                    wait_full(act, f"qt{c}")
                    if c:
                        wait_full(act, f"sc{c - 1}")
                    made(copy(W[8][:], bank(f"qt{c}")[:]), "qT")
                if k % 2 == 0 and 0 <= (k - 2) // 2 < 4:
                    c = (k - 2) // 2
                    wait_full(act, f"q{c}")
                    if c:
                        wait_full(act, f"qt{c - 1}")
                    made(copy(W[6][:], bank(f"q{c}")[:]), "q_tm")
            yield "gate1"
            act.wait_ge(sig("g_sub"), 1)
            made(S.activation(g_next[:], g_next[:], ACT.Exp), "g_exp")

        def mix_vector(dve, b, step, seen, chain):
            keys = slice(0, seen * P)

            def tt(out, in0, in1, op=ALU.mult):
                return V.tensor_tensor(out, in0, in1, op)

            def over(scalars, n):
                return scalars.unsqueeze(2).to_broadcast([P, scalars.shape[1], n])

            def mean(n, width):
                dve.wait_ge(sig("squares" + n), 1)
                made(V.tensor_scalar(sm["ms" + n][:], sm["ss" + n][:], 1.0 / width, EPS, ALU.mult, ALU.add), "mean" + n)

            def rstd(n):
                dve.wait_ge(sig("root" + n), 1)
                chain(V.reciprocal(sm["rs" + n][:], sm["rt" + n][:]))

            Xb = X[:, bass.ds(b, 1), :].rearrange("p o d -> p (o d)")
            yield "n1a"
            carry = const_at("carry", step, 1)
            made(V.tensor_scalar(state[:], state[:], carry, None, ALU.mult), "state_kept")
            chain(V.tensor_scalar(xbcT[:, :, 0:TAPS - 1], xbcT[:, :, 0:TAPS - 1], carry, None, ALU.mult))
            chain(V.tensor_copy(rope[:].rearrange("p a d -> p (a d)"), const_at("rope", b * 16, 16)))
            yield "n1b"
            mean("1", D)
            yield "n1d"
            rstd("1")
            made(V.tensor_scalar(mix[:], Xb, sm["rs1"][:], None, ALU.mult), "normed1")
            yield "n1e"
            for half in range(2):
                use = f"h_t{half}"
                wait_full(dve, use)
                dve.wait_ge(sig("n1w_in"), 16)
                made(tt(hT[:, 4 * half:4 * half + 4], bank(use)[:].rearrange("p (k t) -> p k t", k=4),
                        over(n1w[:, 4 * half:4 * half + 4], P)), "hT")
            conv = scratch[:].rearrange("p (i t) -> p i t", i=8)
            for t in range(TAPS):
                yield f"conv{t}"
                if t == 0:
                    dve.wait_ge(sig("xbc_in"), 2)
                    dve.wait_ge(sig("params_out"), 1)
                for i in range(8):
                    tap = conv_p[:, t * 8 + i:t * 8 + i + 1]
                    if t == 0:
                        ins = V.tensor_scalar(conv[:, i], xbcT[:, i, 0:P], tap, conv_p[:, 32 + i:33 + i], ALU.mult, ALU.add)
                    else:
                        dve.wait_ge(sig("conv"), 8 * (t - 1) + i + 1)
                        ins = V.scalar_tensor_tensor(conv[:, i], xbcT[:, i, t:t + P], tap, conv[:, i], ALU.mult, ALU.add)
                    made(ins, "conv")
            yield "conv_out"
            dve.wait_ge(sig("conv"), 8 * TAPS)
            chain(V.tensor_copy(xbcT[:, :, 0:TAPS - 1], xbcT[:, :, P:P + TAPS - 1]))
            yield "kv0"
            dve.wait_ge(sig("params_in"), 16 * PARAMS)
            wait_full(dve, "vq")
            made(V.tensor_copy(sbv[:, bass.ds(b, 1), :].rearrange("p o d -> p (o d)"), bank("vq")[:, 0:256]), "sb_v")
            made(V.tensor_copy(nqk[:, 3:7, :].rearrange("p h d -> p (h d)"), bank("vq")[:, 256:512]), "vq_read")
            dve.wait_ge(sig("vq_read"), 1)
            xs_tm = W[1][:].rearrange("p (h d) -> p h d", d=HD)
            x_dt, x_dec = (W[n][:].rearrange("p (h d) -> p h d", d=HD) for n in (2, 3))
            y = W[6][:].rearrange("p (h d) -> p h d", d=HD)

            def ssd(k):
                if k == 0:
                    wait_full(dve, "kv")
                    pairs = bank("kv")[:, 8:8 + 6 * HD].rearrange("p (i a d) -> p i a d", a=2, d=HD)
                    chain(V.tensor_copy(nqk[:, 0:3, :], pairs[:, :, 0]))
                    chain(V.tensor_copy(kcvc[:, 1], pairs[:, 0, 1]))
                    chain(V.tensor_copy(nsv[:, bass.ds(b, 1), :].rearrange("p o (a d) -> p (o a) d", a=2), pairs[:, 1:3, 1]))
                    chain(V.tensor_copy(sm["gt"][:], bank("kv")[:, 8 + 6 * HD:8 + KVW]))
                    made(tt(sm["dtp"][:], bank("kv")[:, 0:8], dtb[:], ALU.add), "kv_read")
                elif k == 2:
                    dve.wait_ge(sig("dt_log"), 1)
                    chain(V.scalar_tensor_tensor(sm["dt"][:], sm["dtp"][:], 0.0, sm["dta"][:], ALU.max, ALU.add))
                    made(V.scalar_tensor_tensor(sm["dtA"][:], sm["dt"][:], -1.0, sm["ea"][:], ALU.mult, ALU.mult), "dtA")
                elif k == 4:
                    wait_full(dve, "cumsum")
                    chain(V.tensor_copy(sm["acs"][:, 0:16], bank("cumsum")[:, 0:16]))
                    chain(V.tensor_scalar(sm["nacs"][:], sm["acs"][:, 0:8], -1.0, None, ALU.mult))
                    made(tt(sm["acs"][:, 16:24], sm["acs"][:, 8:16], sm["acs"][:, 0:8], ALU.subtract), "acs")
                elif k == 5:
                    dve.wait_ge(sig("xs_tm"), 1)
                    made(tt(x_dt, xs_tm, over(sm["dt"][:], HD)), "x_dt")
                elif k == 6:
                    dve.wait_ge(sig("x_dt"), 1)
                    dve.wait_ge(sig("ed"), 1)
                    made(tt(x_dec, x_dt, over(sm["ed"][:, 16:24], HD)), "x_dec")
                elif k == 7:
                    wait_full(dve, "cb")
                    dve.wait_ge(sig("decay"), 2)
                    for g in range(2):
                        m = W[4 + g][:].rearrange("p (h l) -> p h l", h=4)
                        made(tt(m, m, bank("cb")[:, g * P:(g + 1) * P].unsqueeze(1).to_broadcast([P, 4, P])), "decayed")
                elif k == 8:
                    wait_full(dve, "y_off")
                    made(tt(y, bank("y_off")[:].rearrange("p (h d) -> p h d", d=HD), over(sm["ed"][:, 0:8], HD)), "y_part")
                    chain(tt(W[7][:].rearrange("p (h d) -> p h d", d=HD), xs_tm, over(dskip[:], HD)))
                    dve.wait_ge(sig("y_part"), 1)
                elif k == 9:
                    chain(tt(W[6][:], W[6][:], W[7][:], ALU.add))
                    wait_full(dve, "y_diag")
                    chain(tt(W[6][:], bank("y_diag")[:], W[6][:], ALU.add))
                    dve.wait_ge(sig("z_silu"), 1)
                    made(tt(W[6][:], W[6][:], W[0][:]), "y")
                elif k == 10:
                    wait_full(dve, "state")
                    s3 = state[:].rearrange("p (h d) -> p h d", d=HD)
                    chain(tt(s3, s3, over(sm["ed"][:, 8:16], HD)))
                    made(tt(state[:], bank("state")[:], state[:], ALU.add), "state_new")
                elif k == 12:
                    mean("2", SSD_W)
                elif k == 14:
                    rstd("2")
                    made(V.tensor_scalar(mix[:, 0:SSD_W], W[6][:], sm["rs2"][:], None, ALU.mult), "mixed_ssd")

            def sb(k):
                if 0 <= k - 2 < SB_H:
                    h = k - 2
                    dve.wait_ge(sig("sb_log"), h + 1)
                    if h >= 2:
                        wait_full(dve, f"sbr{h - 2}")
                    sp = sb_sp[h % 2][:, keys]
                    chain(tt(sp, sb_relu[h % 2][:, keys], sb_ln[h % 2][:, keys], ALU.add))
                    made(tt(sp, sp, const_at("stay", (BLOCKS - 1 - b) * P, seen * P)), "softplus")
                elif k == 10:
                    mean("3", 256)
                elif k == 12:
                    rstd("3")
                    made(V.tensor_scalar(mix[:, SSD_W:SSD_W + 256], bank("sb_o")[:, 0:256], sm["rs3"][:], None, ALU.mult), "mixed_sb")

            def nsa_qk(k):
                if k == 2:
                    sq = W[7][:, 0:384].rearrange("p (h d) -> p h d", d=HD)
                    chain(tt(sq, nqk[:, 1:7], nqk[:, 1:7]))
                    V.tensor_reduce(sm["ssq"][:], sq, AX.X, ALU.add).then_inc(sig("squaresq"), 1)
                    mean("q", HD)
                elif k == 6:
                    rstd("q")
                    chain(tt(nqk[:, 1:7], nqk[:, 1:7], over(sm["rsq"][:], HD)))
                    chain(tt(nqk[:, 1:7], nqk[:, 1:7], qkw[:, 1:7]))
                    chain(V.tensor_scalar(sm["sg"][:], sm["sg"][:], 1.0, None, ALU.add))
                    chain(V.reciprocal(sm["sg"][:], sm["sg"][:]))
                elif k == 11:
                    x1, x2 = nqk[:, :, 0:8], nqk[:, :, 8:16]
                    cos, sin = (rope[:, i, :].unsqueeze(1).to_broadcast([P, 7, 8]) for i in range(2))
                    chain(tt(r[:, 0], x1, cos))
                    chain(tt(r[:, 1], x2, sin))
                    chain(tt(r[:, 2], x2, cos))
                    chain(tt(r[:, 3], x1, sin))
                    chain(tt(x1, r[:, 0], r[:, 1], ALU.subtract))
                    chain(tt(x2, r[:, 2], r[:, 3], ALU.add))
                elif k == 13:
                    chain(V.tensor_copy(kcvc[:, 0], nqk[:, 0]))
                    chain(V.tensor_copy(kk[:, :, 0], nqk[:, 1:3]))
                    made(V.tensor_copy(kk[:, :, 1], nqk[:, 1:3]), "roped")

            for k in range(A_PHASES):
                yield f"a{k}"
                sb(k)
                ssd(k)
                nsa_qk(k)
            yield "ne"
            wait_full(dve, "n_t")
            dve.wait_ge(sig("nqT"), 1)
            made(V.tensor_copy(nkT[:, :, bass.ds(b * P, P)], bank("n_t")[:, 256:512].rearrange("p (a t) -> p a t", a=2)), "nkT")
            wait_full(dve, "kcvc_t")
            made(V.tensor_copy(kcvcT[:, bass.ds(b * P, P)], bank("kcvc_t")[:, 0:P]), "kcvcT")
            yield "cmp_z"
            dve.wait_ge(sig("kcvcT"), 1)
            by_block = kcvcT[:].rearrange("p (c j) -> p j c", j=CMP_STRIDE)
            for half in range(2):
                js = slice(CMP_STRIDE * half, CMP_STRIDE * (half + 1))
                ins = tt(cmp_z[:, js], by_block[:, :, half:half + CMP_PAD], posT[:, js].unsqueeze(2).to_broadcast([P, CMP_STRIDE, CMP_PAD]),
                         ALU.add)
                if half:
                    made(ins, "cmp_z")
                else:
                    chain(ins)
            head_of = const("head_of")
            o = W[0][:, 0:256].rearrange("p (h d) -> p h d", d=HD)
            gates = sm["sg"][:].rearrange("p (h b) -> p b h", b=3)

            def compressed(k):
                if k == 0:
                    for kv, use in enumerate(("cmp_k", "cmp_v")):
                        wait_full(dve, use)
                        made(V.tensor_copy(W[6][0:64, kv * P:(kv + 1) * P].rearrange("p (a c) -> p a c", a=4),
                                           bank(use)[0:64, 0:CMP_PAD].unsqueeze(1).to_broadcast([64, 4, CMP_PAD])), "cmp_rep")
                elif k == 2:
                    wait_full(dve, "cmp_tt")
                    chain(V.tensor_copy(kn[:], bank("cmp_tt")[:, 0:HD]))
                    chain(tt(W[9][:, 256:320], kn[:], kn[:]))
                    V.tensor_reduce(sm["ssc"][:], W[9][:, 256:320], AX.X, ALU.add).then_inc(sig("squaresc"), 1)
                    mean("c", HD)
                    made(tt(W[9][:, 0:256].rearrange("p (h d) -> p h d", d=HD),
                            bank("cmp_tt")[:, HD:2 * HD].unsqueeze(1).to_broadcast([P, 4, HD]), over(head_of, HD)), "v_bd")
                elif k == 4:
                    rstd("c")
                    chain(V.tensor_scalar(kn[:], kn[:], sm["rsc"][:], None, ALU.mult))
                    chain(tt(kn[:], kn[:], qkw[:, 0]))
                    made(tt(k2[:], kn[0:64].unsqueeze(1).to_broadcast([64, 2, HD]),
                            head_of[0:64, 0:2].unsqueeze(2).to_broadcast([64, 2, HD])), "k2")
                elif k == 8:
                    wait_full(dve, "cmp_s")
                    sc = bank("cmp_s")[:, 0:P].rearrange("p (h c) -> p h c", h=4)
                    chain(V.tensor_reduce(sm["cm"][:], sc, AX.X, ALU.max))
                    made(tt(W[7][:, 0:P].rearrange("p (h c) -> p h c", h=4), sc, over(sm["cm"][:], CMP_PAD), ALU.subtract), "cmp_sub")
                elif k == 10:
                    pc = W[7][:, 0:P].rearrange("p (h c) -> p h c", h=4)
                    dve.wait_ge(sig("cmp_e"), 1)
                    chain(V.tensor_reduce(sm["csum"][:], pc[:, :, 0:CMP_PAD - 1], AX.X, ALU.add))
                    chain(V.reciprocal(sm["crec"][:], sm["csum"][:]))
                    chain(tt(pc, pc, over(sm["crec"][:], CMP_PAD)))
                    made(tt(W[7][:, 0:P], W[7][:, 0:P], const_at("cmp_seen", b * P, P)), "cmp_p")
                elif k == 14:
                    wait_full(dve, "cmp_o")
                    made(tt(o, bank("cmp_o")[:, 0:256].rearrange("p (h d) -> p h d", d=HD), over(gates[:, 0], HD)), "o_cmp")

            for k in range(T_PHASES):
                yield f"t{k}"
                if 0 <= k - 1 < 2 * NSA_H:
                    i = k - 1
                    wait_full(dve, f"s{i}")
                    chain(V.reduce_max(sm["mx"][:, i:i + 1], bank(f"s{i}")[:, keys], AX.X))
                    made(V.tensor_scalar(sm["nm"][:, i:i + 1], sm["mx"][:, i:i + 1], -1.0, None, ALU.mult), "row_max")
                compressed(k)
            yield "nsum0"
            dve.wait_ge(sig("o_cmp"), 1)
            dve.wait_ge(sig("probs"), 2 * NSA_H)
            chain(V.reciprocal(sm["coef"][:], sm["sums"][:]))
            cf = sm["coef"][:].rearrange("p (b h) -> p b h", b=2)
            chain(tt(cf, cf, gates[:, 1:3]))
            wait_full(dve, "att_o")
            made(tt(W[1][:].rearrange("p (h d) -> p h d", d=HD), bank("att_o")[:].rearrange("p (h d) -> p h d", d=HD),
                    over(sm["coef"][:], HD)), "att_read")
            dve.wait_ge(sig("att_read"), 1)
            chain(tt(W[0][:, 0:256], W[0][:, 0:256], W[1][:, 0:256], ALU.add))
            made(tt(W[0][:, 0:256], W[0][:, 0:256], W[1][:, 256:512], ALU.add), "nsa_o")
            yield "nsum2"
            mean("4", 256)
            yield "nsum4"
            rstd("4")
            made(V.tensor_scalar(mix[:, SSD_W + 256:], W[0][:, 0:256], sm["rs4"][:], None, ALU.mult), "mixed_nsa")
            yield "me"
            for half in range(2):
                use = f"mix_t{half}"
                wait_full(dve, use)
                made(tt(hT[:, 4 * half:4 * half + 4], bank(use)[:].rearrange("p (k t) -> p k t", k=4),
                        over(catw[:, 4 * half:4 * half + 4], P)), "mixT")
            for half, phase in enumerate(("out2", "oe")):
                yield phase
                wait_full(dve, f"out{half}")
                xh = X[:, bass.ds(b, 1), half * 512:(half + 1) * 512].rearrange("p o d -> p (o d)")
                made(tt(xh, bank(f"out{half}")[:], xh, ALU.add), "x_mid")
            yield "n2b"
            mean("5", D)
            yield "n2d"
            rstd("5")
            made(V.scalar_tensor_tensor(h2_next[:], Xb, sm["rs5"][:], n2w[:], ALU.mult, ALU.mult), "normed2")

            picks = [0] * 3

            def top16(rows):
                def step(i, ins):
                    made(ins, f"pick{i}")
                    picks[i] += 1

                def last(i):
                    dve.wait_ge(sig(f"pick{i}"), picks[i])

                for i, (src, work, values, indices) in enumerate(rows):
                    step(i, V.max(values[:, 0:8], src))
                for i, (src, work, values, indices) in enumerate(rows):
                    last(i)
                    step(i, V.max_index(indices[:, 0:8], values[:, 0:8], src))
                for i, (src, work, values, indices) in enumerate(rows):
                    last(i)
                    step(i, V.match_replace(work, values[:, 0:8], src, -3.0e38))
                for i, (src, work, values, indices) in enumerate(rows):
                    last(i)
                    step(i, V.max(values[:, 8:16], work))
                for i, (src, work, values, indices) in enumerate(rows):
                    last(i)
                    step(i, V.max_index(indices[:, 8:16], values[:, 8:16], work))
                for i in range(len(rows)):
                    last(i)

            for k in range(R_PHASES):
                yield f"r{k}"
                c, half = (k - 7) // 2, (k - 7) % 2
                h = k - 9
                picking = []
                if 0 <= c < 4:
                    dve.wait_ge(sig("scores"), c + 1)
                    for i in (2 * half, 2 * half + 1):
                        picking.append((W[c % 2][:, i * P:(i + 1) * P], W[9][:, i % 2 * P:(i % 2 + 1) * P],
                                        sv[:, 4 * c + i], si[:, 4 * c + i]))
                if 0 <= h < PEER_H:
                    cand = W[2][:, 0:256]
                    chain(tt(cand.rearrange("p (i j) -> p i j", i=TOPK), sv[:, 2 * h].unsqueeze(2).to_broadcast([P, TOPK, TOPK]),
                             sv[:, 2 * h + 1].unsqueeze(1).to_broadcast([P, TOPK, TOPK]), ALU.add))
                    picking.append((cand, W[3][:, 0:256], cv[:, h], ci[:, TOPK * h:TOPK * (h + 1)]))
                top16(picking)
                if 0 <= c < 4 and half:
                    made(V.tensor_copy(sif[:, 4 * c:4 * c + 4], si[:, 4 * c:4 * c + 4]), "top_keys")
            chosen = sif[:].rearrange("p (h a) k -> p a h k", a=2)
            n = SLOTS // 4
            for part in range(8):
                yield f"dec{part}"
                if part == 0:
                    dve.wait_ge(sig("top_keys"), 4)
                    chain(V.tensor_scalar(ch[:, 0], ci[:], 4, None, ALU.logical_shift_right))
                    chain(V.tensor_scalar(ch[:, 1], ci[:], TOPK - 1, None, ALU.bitwise_and))
                    chain(V.tensor_copy(chf[:], ch[:]))
                half, quarter = part // 4, part % 4
                eq = W[4][:].rearrange("p (s k) -> p s k", k=TOPK)
                chain(tt(eq, chf[:, half, n * quarter:n * (quarter + 1)].unsqueeze(2).to_broadcast([P, n, TOPK]),
                         iota16.unsqueeze(1).to_broadcast([P, n, TOPK]), ALU.is_equal))
                e4 = W[4][:].rearrange("p (h s k) -> p h s k", h=2, k=TOPK)
                chain(tt(e4, e4, chosen[:, half, 2 * quarter:2 * quarter + 2].unsqueeze(2).to_broadcast([P, 2, TOPK, TOPK])))
                chain(V.tensor_reduce(picked[:, half, n * quarter:n * (quarter + 1)], eq, AX.X, ALU.add))
            yield "gate0"
            chain(V.scalar_tensor_tensor(picked[:, 1], picked[:, 0], float(KEYS), picked[:, 1], ALU.mult, ALU.add))
            chain(V.tensor_scalar(idx_next[:], picked[:, 1], const_at("first_row", step, 1), None, ALU.add))
            g3 = g_next[:].rearrange("p (h k) -> p h k", k=TOPK)
            made(tt(g3, cv[:], cv[:, :, 0:1].to_broadcast([P, PEER_H, TOPK]), ALU.subtract), "g_sub")
            yield "gate2"
            dve.wait_ge(sig("g_exp"), 1)
            chain(V.tensor_reduce(sm["gsum"][:], g3, AX.X, ALU.add))
            chain(V.reciprocal(sm["grec"][:], sm["gsum"][:]))
            chain(tt(g3, g3, over(sm["grec"][:], TOPK)))

        class Phases:

            def __init__(self, part):
                self.part, self.at = part, next(part)

            def upto(self, last):
                while self.at is not None and ORDER[self.at] <= last:
                    before, self.at = self.at, next(self.part, None)
                    assert self.at is None or ORDER[self.at] > ORDER[before], (before, self.at)

        def phase_after(slot):
            return int((WORK * PACE <= SPARE[slot]).sum()) - 1

        def of_vector(s):
            return BY_VECTOR[s]

        def before(s):
            vector = sum(BY_VECTOR[:s + 1])
            return s + 1 - vector, vector

        def wait_added(eng, s):
            tensor, vector = before(s)
            if of_vector(s):
                eng.wait_ge(sig("v_used_vector"), vector)
            else:
                eng.wait_ge(sig("v_used"), tensor)

        def started(eng):
            eng.wait_ge(sig("start_in"), 32)
            eng.wait_ge(sig("caches_zero"), 7)

        def step_program(mixing, gathering):
            seen = 1 if gathering is None else BLOCKS
            with nc.Block() as block:
                @block.sync
                def _(sp):
                    if gathering is None:
                        x_blocks = x_dram.rearrange("o (b p) d -> (o p) b d", p=P)
                        sp.dma_start(X[:, 0:1], x_blocks[:, 0:1]).then_inc(sig("start_in"), 16)
                        sp.dma_start(consts[:], const_dram).then_inc(sig("start_in"), 16)
                    if mixing:
                        mix_sync(sp, mixing[2])
                    else:
                        sp.dma_start(out_blocks[:, 0:BLOCKS - 1], X[:, 0:BLOCKS - 1]).then_inc(sig("out_early"), 16)
                        sp.wait_ge(sig("out_early"), 16)
                    if gathering is None:
                        sp.dma_start(X[:, 1:], x_blocks[:, 1:]).then_inc(sig("x_in"), 16)
                        sp.wait_ge(sig("x_in"), 16)

                @block.gpsimd
                def _(pool):
                    if gathering is None:
                        for tile in (state, xbcT, sbkT, sbv, nkT, nsv, kcvcT):
                            made(pool.memset(tile[:], 0.0), "caches_zero")
                        return
                    pool.wait_ge(sig("idx_now"), 1)
                    for t in range(SLOTS + LAG):
                        if t < SLOTS:
                            if t >= U_RING:
                                pool.wait_ge(sig("u_used"), t - U_RING + 1)
                            pool.indirect_dma_start(
                                out=u_rows[:, t % U_RING, :], out_offset=None, in_=a["peer_u"],
                                in_offset=bass.IndirectOffsetOnAxis(ap=idx_now[:, t:t + 1], axis=0),
                            ).then_inc(u_in[t % U_RING], 16)
                        if t >= LAG:
                            s = t - LAG
                            if s >= V_RING:
                                wait_added(pool, s - V_RING)
                            pool.indirect_dma_start(
                                out=v_rows[:, s % V_RING, :], out_offset=None, in_=a["peer_v"],
                                in_offset=bass.IndirectOffsetOnAxis(ap=idx_now[:, s:s + 1], axis=0),
                            ).then_inc(v_in[s % V_RING], 16)

                @block.vector
                def _(dve):
                    chain = InOrder(dve, sig("vector_chain"))
                    phases = mixing and Phases(mix_vector(dve, mixing[1], mixing[0], seen, chain))
                    if gathering is None:
                        started(dve)
                        phases.upto(len(PHASES))
                        return
                    made(V.tensor_copy(idx_now[:], idx_next[:]), "idx_now")
                    chain(V.tensor_copy(g_now[:], g_next[:]))
                    chain(V.tensor_copy(h2_now[:], h2_next[:]))
                    made(V.memset(acc_v[:], 0.0), "v_used_zero")
                    for s in range(SLOTS + LAG):
                        if s < SLOTS:
                            dve.wait_ge(u_in[s % U_RING], 16 * (s // U_RING + 1))
                            rows_u = u_rows[:, s % U_RING, :]
                            made(V.tensor_tensor_reduce(out=rows_u, in0=rows_u, in1=h2_now[:], scale=1.0, scalar=0.0,
                                                        op0=ALU.mult, op1=ALU.add, accum_out=dots[:, s:s + 1]), "u_used")
                        if s % TOPK == 1 and TOPK < s < SLOTS + TOPK:
                            head = s // TOPK - 1
                            dve.wait_ge(sig("gelu"), head + 1)
                            cols = slice(head * TOPK, (head + 1) * TOPK)
                            made(V.tensor_tensor(wgt[:, cols], gel[:, cols], g_now[:, cols], ALU.mult), "weights")
                        t = s - LAG
                        if t >= 0 and of_vector(t):
                            dve.wait_ge(v_in[t % V_RING], 16 * (t // V_RING + 1))
                            dve.wait_ge(sig("weights"), t // TOPK + 1)
                            if before(t)[1] > 1:
                                dve.wait_ge(sig("v_used_vector"), before(t)[1] - 1)
                            else:
                                dve.wait_ge(sig("v_used_zero"), 1)
                            made(V.scalar_tensor_tensor(acc_v[:], v_rows[:, t % V_RING, :], wgt[:, t:t + 1], acc_v[:],
                                                        ALU.mult, ALU.add), "v_used_vector")
                        if mixing:
                            phases.upto(phase_after(s))
                    wait_added(dve, SLOTS - 2)
                    wait_added(dve, SLOTS - 1)
                    chain(V.tensor_tensor(X[:, bass.ds(gathering, 1), :].rearrange("p o d -> p (o d)"), acc[:], acc_v[:], ALU.add))

                @block.scalar
                def _(act):
                    chain = InOrder(act, sig("scalar_chain"))
                    phases = mixing and Phases(mix_scalar(act, mixing[1], seen, chain))
                    if gathering is None:
                        started(act)
                        phases.upto(len(PHASES))
                        return
                    for s in range(SLOTS + LAG):
                        if s % TOPK == 0 and s > 0 and s <= SLOTS:
                            head = s // TOPK - 1
                            act.wait_ge(sig("u_used"), TOPK * (head + 1))
                            cols = slice(head * TOPK, (head + 1) * TOPK)
                            made(S.activation(gel[:, cols], dots[:, cols], ACT.Gelu), "gelu")
                        t = s - LAG
                        if t >= 0 and not of_vector(t):
                            n = before(t)[0] - 1
                            act.wait_ge(sig("weights"), t // TOPK + 1)
                            if n >= DIAG_RING:
                                act.wait_ge(sig("v_used"), n - DIAG_RING + 1)
                            made(S.activation(diag[:, n % DIAG_RING], ident, ACT.Copy, scale=wgt[:, t:t + 1]), "diag")
                        if mixing:
                            phases.upto(phase_after(s))

                @block.tensor
                def _(pe):
                    phases = mixing and Phases(mix_tensor(pe, mixing[1], seen))
                    if gathering is None:
                        started(pe)
                        phases.upto(len(PHASES))
                        return
                    for half in range(2):
                        T.matmul(acc[:, half * 512:(half + 1) * 512], ident,
                                 X[:, bass.ds(gathering, 1), half * 512:(half + 1) * 512].rearrange("p o d -> p (o d)"),
                                 start=True, stop=False)
                    for s in range(SLOTS + LAG):
                        t = s - LAG
                        if t >= 0 and not of_vector(t):
                            n = before(t)[0] - 1
                            pe.wait_ge(sig("diag"), n + 1)
                            pe.wait_ge(v_in[t % V_RING], 16 * (t // V_RING + 1))
                            for half in range(2):
                                last = T.matmul(acc[:, half * 512:(half + 1) * 512], diag[:, n % DIAG_RING],
                                                v_rows[:, t % V_RING, half * 512:(half + 1) * 512],
                                                start=False, stop=(t == SLOTS - 2))
                            made(last, "v_used")
                        if mixing:
                            phases.upto(phase_after(s))

        def clear():
            numbers = sorted(s.num for s in sems.values())
            assert numbers == list(range(numbers[0], numbers[0] + len(numbers)))
            nc.gpsimd.dma_reset(range(numbers[0], numbers[-1] + 1))
            nc.gpsimd.sem_clear(range(numbers[0], numbers[-1] + 1))
            nc.all_engine_barrier()

        out_blocks = out_dram.rearrange("o (b p) d -> (o p) b d", p=P)
        step_program((0, 0, 0), None)
        clear()
        with nc.Fori(0, STEPS - 1) as n:
            step_program((n + 1, (n + 1) % BLOCKS, (n + 1) // BLOCKS), n % BLOCKS)
            clear()
        step_program(None, BLOCKS - 1)
        with nc.Block() as block:
            @block.sync
            def _(sp):
                sp.dma_start(out_blocks[:, BLOCKS - 1:], X[:, BLOCKS - 1:]).then_inc(sig("out_done"), 16)
                sp.wait_ge(sig("out_done"), 16)


_INS = ["x", "norm1_w", "w_in", "conv_w", "conv_b", "dt_bias", "a_log", "d_skip", "ssd_norm_w", "sb_out_w",
        "nsa_q_norm_w", "nsa_k_norm_w", "nsa_cmp_pos", "nsa_cmp_w", "nsa_out_w", "w_out", "norm2_w",
        "peer_w_q", "peer_sub_keys", "peer_u", "peer_v"]


def kernel(**inputs):
    import concourse.bacc as bacc
    from concourse.bass_utils import run_bass_kernel_spmd as run

    nc = bacc.Bacc("TRN2", target_bir_lowering=False, num_devices=1)
    arrays, aps = {}, {}
    for name in _INS:
        v = np.ascontiguousarray(inputs[name])
        if name in ("peer_u", "peer_v"):
            v = v.reshape(DEPTH * EXPERTS, D)
        arrays["in_" + name] = v
        aps[name] = nc.dram_tensor("in_" + name, v.shape, mybir.dt.float32, kind="ExternalInput").ap()
    arrays["constants"] = constants()
    const_dram = nc.dram_tensor("constants", arrays["constants"].shape, mybir.dt.float32, kind="ExternalInput").ap()
    out = nc.dram_tensor("out", (1, SEQ, D), mybir.dt.float32, kind="ExternalOutput").ap()
    trunk(nc, aps, const_dram, aps["x"], out)
    r = run(nc, [arrays], core_ids=[0])
    return r.results[0]["out"]
```
